# Optimizing a Trainium2 kernel written in Bass

```python
import math
import jax, jax.numpy as jnp
from jax import lax
import numpy as np

D_MODEL = 1024
BATCH = 1
SEQ = 256
DEPTH = 2
DEC_BATCH = 8
DEC_SEQ = 1
PAST_LEN = 2048
PAGE_SIZE = 128

D_MIX = D_MODEL
W_A = D_MIX // 4
G_A = 4
CONV_A = 31
W_B = D_MIX // 2
H_B = 4
DH_B = W_B // H_B
CONV_B = 4
MLSTM_CHUNK = 64
W_C = D_MIX // 4
H_C = 4
DH_C = W_C // H_C
CONV_C = 4
RG_C = 8.0
D_IN = 2 * W_A + 2 * W_B + 2 * W_C
SPLITS = [W_A, 2 * W_A, 2 * W_A + W_B, 2 * W_A + 2 * W_B, 2 * W_A + 2 * W_B + W_C]
D_FF = 11 * D_MODEL // 4
N_EXPERTS = 8
TOP_K = 2
D_FF_EXPERT = D_FF // 2
N_DENSE = (DEPTH + 1) // 2
N_MOE = DEPTH // 2
NORM_EPS = 1e-6
LN_EPS = 1e-5

kernel_name = 'hymba_conformer_mlstm_rglru_moe_step'

def rmsnorm(x, g):
    xf = x.astype(jnp.float32)
    y = xf * lax.rsqrt(jnp.mean(xf * xf, axis=-1, keepdims=True) + NORM_EPS)
    return (y * g.astype(jnp.float32)).astype(x.dtype)

def group_layernorm(x, g, b, groups):
    shp = x.shape
    xf = x.astype(jnp.float32).reshape(shp[:-1] + (groups, shp[-1] // groups))
    mu = jnp.mean(xf, axis=-1, keepdims=True)
    var = jnp.mean(jnp.square(xf - mu), axis=-1, keepdims=True)
    y = ((xf - mu) * lax.rsqrt(var + LN_EPS)).reshape(shp)
    return (y * g.astype(jnp.float32) + b.astype(jnp.float32)).astype(x.dtype)

def head_layernorm(h, g):
    mu = jnp.mean(h, axis=-1, keepdims=True)
    var = jnp.mean(jnp.square(h - mu), axis=-1, keepdims=True)
    return (h - mu) * lax.rsqrt(var + LN_EPS) * g.astype(jnp.float32).reshape(h.shape[-2:])

def causal_dwconv(x, buf, w, b):
    xp = jnp.concatenate([buf.astype(x.dtype), x], axis=1)
    k = w.shape[0]
    y = lax.conv_general_dilated(xp, w[:, None, :].astype(x.dtype), window_strides=(1,), padding='VALID',
                                 dimension_numbers=('NWC', 'WIO', 'NWC'), feature_group_count=x.shape[-1])
    return y + b, xp[:, xp.shape[1] - (k - 1):]

def headwise(x, w):
    bn, l, _ = x.shape
    return jnp.einsum('blhi,hij->blhj', x.reshape(bn, l, w.shape[0], w.shape[1]), w)

def _mlstm_chunk_step(carry, chunk):
    C, n, m = carry
    q, k, v, ig, lf = chunk
    L = q.shape[1]
    b = jnp.cumsum(lf, axis=1)
    causal = jnp.tril(jnp.ones((L, L), dtype=bool))
    dmat = b[:, :, None, :] - b[:, None, :, :] + ig[:, None, :, :]
    dmat = jnp.where(causal[None, :, :, None], dmat, -jnp.inf)
    inter = b + m[:, None, :]
    m_t = jnp.maximum(inter, jnp.max(dmat, axis=2))
    s = jnp.einsum('bthd,bshd->btsh', q, k) * jnp.exp(dmat - m_t[:, :, None, :])
    w_inter = jnp.exp(inter - m_t)
    num = jnp.einsum('btsh,bshd->bthd', s, v) + w_inter[..., None] * jnp.einsum('bthk,bhkv->bthv', q, C)
    den = jnp.sum(s, axis=2) + w_inter * jnp.einsum('bthk,bhk->bth', q, n)
    h = num / jnp.maximum(jnp.abs(den), jnp.exp(-m_t))[..., None]
    m_new = m_t[:, -1]
    g = jnp.exp(b[:, -1:, :] - b + ig - m_new[:, None, :])
    decay = jnp.exp(b[:, -1] + m - m_new)
    C_new = decay[..., None, None] * C + jnp.einsum('bsh,bshk,bshv->bhkv', g, k, v)
    n_new = decay[..., None] * n + jnp.einsum('bsh,bshk->bhk', g, k)
    return (C_new, n_new, m_new), h

def mlstm_chunkwise(q, k, v, ig, lf, C, n, m):
    bn, L = q.shape[:2]
    chunk = MLSTM_CHUNK if L % MLSTM_CHUNK == 0 else L
    nc = L // chunk

    def to_chunks(t):
        return jnp.moveaxis(t.reshape((bn, nc, chunk) + t.shape[2:]), 1, 0)

    (C, n, m), hs = lax.scan(_mlstm_chunk_step, (C, n, m),
                             (to_chunks(q), to_chunks(k), to_chunks(v), to_chunks(ig), to_chunks(lf)))
    h = jnp.moveaxis(hs, 0, 1).reshape((bn, L) + hs.shape[3:])
    return h, C, n, m

def rglru(x, h0, w_ra, b_ra, w_ix, b_ix, lam):
    bn, L, _ = x.shape
    r = jax.nn.sigmoid((headwise(x, w_ra).reshape(bn, L, W_C) + b_ra).astype(jnp.float32))
    i = jax.nn.sigmoid((headwise(x, w_ix).reshape(bn, L, W_C) + b_ix).astype(jnp.float32))
    log_a = RG_C * r * jax.nn.log_sigmoid(lam.astype(jnp.float32))
    a = jnp.exp(log_a)
    u = jnp.sqrt(-jnp.expm1(2.0 * log_a)) * i * x.astype(jnp.float32)

    def combine(e1, e2):
        a1, u1 = e1
        a2, u2 = e2
        return a1 * a2, a2 * u1 + u2

    a_cum, u_cum = lax.associative_scan(combine, (a, u), axis=1)
    h = a_cum * h0[:, None, :] + u_cum
    return h, h[:, -1]

def token_mixers(h, st, p, l):
    buf_a, buf_b, C0, n0, m0, buf_c, hc0 = st
    bn, L, _ = h.shape
    f32 = jnp.float32
    u = h @ p['w_in'][l]
    xa, ga, xb, zb, xc, gc = jnp.split(u, SPLITS, axis=-1)
    a = xa * jax.nn.sigmoid(ga)
    a, new_buf_a = causal_dwconv(a, buf_a, p['conv_a_w'][l], p['conv_a_b'][l])
    a_out = jax.nn.silu(group_layernorm(a, p['ln_a_g'][l], p['ln_a_b'][l], G_A))
    cb, new_buf_b = causal_dwconv(xb, buf_b, p['conv_b_w'][l], p['conv_b_b'][l])
    cb = jax.nn.silu(cb)
    q = headwise(cb, p['w_q'][l])
    k = headwise(cb, p['w_k'][l]) * (DH_B ** -0.5)
    v = headwise(xb, p['w_v'][l])
    qkv = jnp.concatenate([q, k, v], axis=-1).reshape(bn, L, 3 * W_B)
    ig = (qkv @ p['w_ig'][l] + p['b_ig'][l]).astype(f32)
    lf = jax.nn.log_sigmoid((qkv @ p['w_fg'][l] + p['b_fg'][l]).astype(f32))
    hb, C1, n1, m1 = mlstm_chunkwise(q.astype(f32), k.astype(f32), v.astype(f32), ig, lf,
                                     C0.astype(f32), n0.astype(f32), m0.astype(f32))
    hb = head_layernorm(hb, p['gn_b_g'][l]).reshape(bn, L, W_B).astype(h.dtype)
    b_out = jax.nn.sigmoid(zb) * (hb + p['skip_b'][l] * cb)
    xcv, new_buf_c = causal_dwconv(xc, buf_c, p['conv_c_w'][l], p['conv_c_b'][l])
    hc, hc1 = rglru(xcv, hc0.astype(f32), p['w_ra'][l], p['b_ra'][l], p['w_ix'][l], p['b_ix'][l], p['lam'][l])
    c_out = hc.astype(h.dtype) * jax.nn.gelu(gc)
    y = jnp.concatenate([a_out, b_out, c_out], axis=-1) @ p['w_out'][l]
    return y, (new_buf_a, new_buf_b, C1, n1, m1, new_buf_c, hc1)

def dense_ffn(h, p, j):
    return (jax.nn.silu(h @ p['w_gate'][j]) * (h @ p['w_up'][j])) @ p['w_down'][j]

def moe_ffn(h, p, j):
    logits = (h @ p['w_router'][j] + p['b_router'][j]).astype(jnp.float32)
    top_v, top_i = lax.top_k(logits, TOP_K)
    gates = jax.nn.softmax(top_v, axis=-1)
    combine = jnp.einsum('blk,blke->ble', gates,
                         jax.nn.one_hot(top_i, N_EXPERTS, dtype=jnp.float32)).astype(h.dtype)
    out = jnp.zeros_like(h)
    for e in range(N_EXPERTS):
        act = jax.nn.silu(h @ p['we_gate'][j, e]) * (h @ p['we_up'][j, e])
        out = out + combine[..., e:e + 1] * (act @ p['we_down'][j, e])
    return out

def trunk(x, states, p):
    new = []
    for l in range(DEPTH):
        st = tuple(s[l] for s in states)
        y, st_new = token_mixers(rmsnorm(x, p['norm_mix_g'][l]), st, p, l)
        x = x + y.astype(x.dtype)
        hn = rmsnorm(x, p['norm_ffn_g'][l])
        f = dense_ffn(hn, p, l // 2) if l % 2 == 0 else moe_ffn(hn, p, l // 2)
        x = x + f.astype(x.dtype)
        new.append(st_new)
    y = rmsnorm(x, p['norm_final_g'])
    new_states = tuple(jnp.stack([s[i] for s in new]).astype(x.dtype) for i in range(7))
    return y, new_states

def setup_inputs(seed: int = 0) -> dict:
    key = jax.random.key(seed)
    ks = iter(jax.random.split(key, 64))
    nrm = lambda shape, s: jax.random.normal(next(ks), shape, jnp.float32) * s
    gain = lambda shape: 1.0 + nrm(shape, 0.02)
    a_init = jax.random.uniform(next(ks), (DEPTH, W_C), jnp.float32, 0.9, 0.999)
    return {
        'x_prompt': nrm((BATCH, SEQ, D_MODEL), 1.0),
        'x_sample': nrm((DEC_BATCH, DEC_SEQ, D_MODEL), 1.0),
        'state_conv_a': nrm((DEPTH, DEC_BATCH, CONV_A - 1, W_A), 0.5),
        'state_conv_b': nrm((DEPTH, DEC_BATCH, CONV_B - 1, W_B), 0.5),
        'state_mlstm_C': nrm((DEPTH, DEC_BATCH, H_B, DH_B, DH_B), 0.05),
        'state_mlstm_n': nrm((DEPTH, DEC_BATCH, H_B, DH_B), 0.5),
        'state_mlstm_m': nrm((DEPTH, DEC_BATCH, H_B), 1.0),
        'state_conv_c': nrm((DEPTH, DEC_BATCH, CONV_C - 1, W_C), 0.5),
        'state_rglru_h': nrm((DEPTH, DEC_BATCH, W_C), 0.5),
        'norm_mix_g': gain((DEPTH, D_MODEL)),
        'w_in': nrm((DEPTH, D_MODEL, D_IN), D_MODEL ** -0.5),
        'conv_a_w': nrm((DEPTH, CONV_A, W_A), CONV_A ** -0.5),
        'conv_a_b': nrm((DEPTH, W_A), 0.02),
        'ln_a_g': gain((DEPTH, W_A)),
        'ln_a_b': nrm((DEPTH, W_A), 0.02),
        'conv_b_w': nrm((DEPTH, CONV_B, W_B), CONV_B ** -0.5),
        'conv_b_b': nrm((DEPTH, W_B), 0.02),
        'w_q': nrm((DEPTH, H_B, DH_B, DH_B), DH_B ** -0.5),
        'w_k': nrm((DEPTH, H_B, DH_B, DH_B), DH_B ** -0.5),
        'w_v': nrm((DEPTH, H_B, DH_B, DH_B), DH_B ** -0.5),
        'w_ig': nrm((DEPTH, 3 * W_B, H_B), 0.3 * (3 * W_B) ** -0.5),
        'b_ig': nrm((DEPTH, H_B), 0.1),
        'w_fg': nrm((DEPTH, 3 * W_B, H_B), 0.3 * (3 * W_B) ** -0.5),
        'b_fg': jnp.linspace(3.0, 6.0, H_B, dtype=jnp.float32)[None, :] + nrm((DEPTH, H_B), 0.1),
        'gn_b_g': gain((DEPTH, W_B)),
        'skip_b': gain((DEPTH, W_B)),
        'conv_c_w': nrm((DEPTH, CONV_C, W_C), CONV_C ** -0.5),
        'conv_c_b': nrm((DEPTH, W_C), 0.02),
        'w_ra': nrm((DEPTH, H_C, DH_C, DH_C), DH_C ** -0.5),
        'b_ra': nrm((DEPTH, W_C), 0.02),
        'w_ix': nrm((DEPTH, H_C, DH_C, DH_C), DH_C ** -0.5),
        'b_ix': nrm((DEPTH, W_C), 0.02),
        'lam': jnp.log(a_init) - jnp.log1p(-a_init),
        'w_out': nrm((DEPTH, D_MIX, D_MODEL), D_MIX ** -0.5),
        'norm_ffn_g': gain((DEPTH, D_MODEL)),
        'w_gate': nrm((N_DENSE, D_MODEL, D_FF), D_MODEL ** -0.5),
        'w_up': nrm((N_DENSE, D_MODEL, D_FF), D_MODEL ** -0.5),
        'w_down': nrm((N_DENSE, D_FF, D_MODEL), D_FF ** -0.5),
        'w_router': nrm((N_MOE, D_MODEL, N_EXPERTS), D_MODEL ** -0.5),
        'b_router': nrm((N_MOE, N_EXPERTS), 0.01),
        'we_gate': nrm((N_MOE, N_EXPERTS, D_MODEL, D_FF_EXPERT), D_MODEL ** -0.5),
        'we_up': nrm((N_MOE, N_EXPERTS, D_MODEL, D_FF_EXPERT), D_MODEL ** -0.5),
        'we_down': nrm((N_MOE, N_EXPERTS, D_FF_EXPERT, D_MODEL), D_FF_EXPERT ** -0.5),
        'norm_final_g': gain((D_MODEL,)),
    }

def reference(x_prompt, x_sample, state_conv_a, state_conv_b, state_mlstm_C, state_mlstm_n, state_mlstm_m,
              state_conv_c, state_rglru_h, norm_mix_g, w_in, conv_a_w, conv_a_b, ln_a_g, ln_a_b,
              conv_b_w, conv_b_b, w_q, w_k, w_v, w_ig, b_ig, w_fg, b_fg, gn_b_g, skip_b,
              conv_c_w, conv_c_b, w_ra, b_ra, w_ix, b_ix, lam, w_out, norm_ffn_g,
              w_gate, w_up, w_down, w_router, b_router, we_gate, we_up, we_down, norm_final_g):
    p = dict(norm_mix_g=norm_mix_g, w_in=w_in, conv_a_w=conv_a_w, conv_a_b=conv_a_b, ln_a_g=ln_a_g,
             ln_a_b=ln_a_b, conv_b_w=conv_b_w, conv_b_b=conv_b_b, w_q=w_q, w_k=w_k, w_v=w_v,
             w_ig=w_ig, b_ig=b_ig, w_fg=w_fg, b_fg=b_fg, gn_b_g=gn_b_g, skip_b=skip_b,
             conv_c_w=conv_c_w, conv_c_b=conv_c_b, w_ra=w_ra, b_ra=b_ra, w_ix=w_ix, b_ix=b_ix, lam=lam,
             w_out=w_out, norm_ffn_g=norm_ffn_g, w_gate=w_gate, w_up=w_up, w_down=w_down,
             w_router=w_router, b_router=b_router, we_gate=we_gate, we_up=we_up, we_down=we_down,
             norm_final_g=norm_final_g)
    bp = x_prompt.shape[0]
    dt = x_prompt.dtype
    zero_states = (jnp.zeros((DEPTH, bp, CONV_A - 1, W_A), dt),
                   jnp.zeros((DEPTH, bp, CONV_B - 1, W_B), dt),
                   jnp.zeros((DEPTH, bp, H_B, DH_B, DH_B), jnp.float32),
                   jnp.zeros((DEPTH, bp, H_B, DH_B), jnp.float32),
                   jnp.zeros((DEPTH, bp, H_B), jnp.float32),
                   jnp.zeros((DEPTH, bp, CONV_C - 1, W_C), dt),
                   jnp.zeros((DEPTH, bp, W_C), jnp.float32))
    y_prompt, new_p = trunk(x_prompt, zero_states, p)
    sample_states = (state_conv_a, state_conv_b, state_mlstm_C, state_mlstm_n, state_mlstm_m,
                     state_conv_c, state_rglru_h)
    y_sample, new_s = trunk(x_sample, sample_states, p)
    conv_a_p, conv_b_p, C_p, n_p, m_p, conv_c_p, h_p = new_p
    conv_a_s, conv_b_s, C_s, n_s, m_s, conv_c_s, h_s = new_s
    return (y_prompt, y_sample, conv_a_p, conv_b_p, C_p, n_p, m_p, conv_c_p, h_p,
            conv_a_s, conv_b_s, C_s, n_s, m_s, conv_c_s, h_s)


_drawn_inputs = setup_inputs


def setup_inputs(seed=0):
    import zlib

    import numpy as np

    out = dict(_drawn_inputs(seed))
    spreads = {}
    factors = {'ln_a_g': 13.97,
     'skip_b': 8.911,
     'b_ra': 8.0,
     'b_ix': 5.351,
     'b_router': 13.265,
     'norm_final_g': 22.516,
     'ln_a_b': 4.488,
     'gn_b_g': 3.994,
     'norm_ffn_g': 5.395}
    for name, (base, spread) in spreads.items():
        noise = np.random.default_rng([zlib.crc32(name.encode()), seed]).standard_normal(out[name].shape)
        drawn = base * np.exp(spread * noise) if base else spread * noise
        out[name] = __import__('jax').numpy.asarray(drawn.astype(out[name].dtype))
    for name, factor in factors.items():
        out[name] = (out[name] * factor).astype(out[name].dtype)
    return out
```

```python
from contextlib import ExitStack

import numpy as np

import concourse.bass as bass
from concourse import mybir

F32, F32R = mybir.dt.float32, mybir.dt.float32r
I32, U32 = mybir.dt.int32, mybir.dt.uint32
ALU, ACT, AX = mybir.AluOpType, mybir.ActivationFunctionType, mybir.AxisListType

P = 128
D = 1024
KT = D // P
TP, NB = 256, 8
T = TP + NB
TILES = [(0, P), (P, P), (TP, NB)]
DEPTH = 2
CA, CB, CC = 31, 4, 4
H = 4
FF = 2816
NE = 8
FE = FF // 2
EPS, LN_EPS = 1e-6, 1e-5
UNIT = 2048
NRAW, NHI = 6, 3
PB = 512
FGW = [512, 512, 384]
NEG = -1.0e30

RA, RB, RC, RN = 34, 31, 40, 5
PA0, PN0 = 0, 2 * 2 * RA
PC0 = PN0 + KT * RN
PS0 = PC0 + 2 * 2 * RC
PEND = PS0 + 2 * NB * H


def dense_groups():
    out = []
    for l in range(DEPTH):
        for g in (0, 1, 3, 2):
            out.append(("w_in", l, 512 * g, 512, [(0, 1, 2, 3), (4, 5, 6, 7)]))
        for g in range(2):
            out.append(("w_out", l, 512 * g, 512, [(0, 1, 6, 7), (2, 3, 4, 5)]))
        if l == 0:
            for g in range(6):
                w = min(512, FF - 512 * g)
                out.append(("w_gate", l, 512 * g, w, [(0, 1, 2, 3), (4, 5, 6, 7)]))
                out.append(("w_up", l, 512 * g, w, [(0, 1, 2, 3), (4, 5, 6, 7)]))
            for g in range(2):
                out.append(("w_down", l, 512 * g, 512, [tuple(range(k, min(k + 4, 22))) for k in range(0, 22, 4)]))
    return out


GROUPS = dense_groups()
UNITS = [(n, l, c0, w, ks) for n, l, c0, w, units in GROUPS for ks in units]
ND = len(UNITS)


def pieces(ks):
    cuts = [0] + [i for i in range(1, len(ks)) if ks[i] != ks[i - 1] + 1] + [len(ks)]
    return list(zip(cuts, cuts[1:]))


def landed(u):
    return 16 * sum(len(pieces(UNITS[v][4])) for v in range(u % NRAW, u + 1, NRAW))


FIRST_UNIT = [sum(len(g[4]) for g in GROUPS[:i]) for i in range(len(GROUPS) + 1)]


SO = [(4, 38, 0, 256), (5, 11, 0, 512), (6, 11, 0, 256), (7, 9, 0, 256), (4, 36, 256, 128)]
NORM_ROW = (0, 2, 1, 3, 4)
TAKEN = [None, 3, 10, 13, None]


def expert_units():
    gate = lambda n, g: [(n, g, 0, 4, FGW[g]), (n, g, 4, 4, FGW[g])]
    down = lambda g: [("down", g, 4 * g + j, min(2, FGW[g] // P - j), D) for j in range(0, FGW[g] // P, 2)]
    return (gate("gate", 0) + gate("up", 0) + gate("gate", 1) + gate("up", 1) + down(0)
            + gate("gate", 2) + gate("up", 2) + down(1) + down(2))


EU = expert_units()
NU = len(EU)
assert NU % NRAW == 0 and ND % NRAW == 0 and NU % NHI == 0 and ND % NHI == 0
POOL_QUARTERS = {u: 1 for u in range(ND) if UNITS[u][0] in ("w_gate", "w_up", "w_down")}
POOL_QUARTERS.update({u: 2 for l in range(DEPTH) for u in range(FIRST_UNIT[20 * l + 4], FIRST_UNIT[20 * l + 4] + 3)})
POOL_UNITS = sorted(POOL_QUARTERS)


HALF0, HALF1 = [2, 12], [1, 11]
LG0, BI0 = 64, 96
COLS0 = 272
POOL_TAPS = 13
DVE_TAPS = (POOL_TAPS, 20, 23, 27, 31)
PRM_DMAS, MIX_DMAS, STORES = 37, 9, 13


def build(nc, a, out):
    ctx = ExitStack()
    with ctx:
        def sem(name):
            return ctx.enter_context(nc.semaphore(name))

        def sb(name, shape, dt=F32, where=ctx):
            return where.enter_context(nc.sbuf_tensor(name, shape, dt))

        with ExitStack() as same:
            low = sb("low", [P, NRAW, UNIT], F32R, where=same)
        raw = sb("raw", [P, NRAW, UNIT])
        whi = sb("whi", [P, NHI, UNIT], F32R)
        xT = sb("xT", [P, KT, T])
        nhi = sb("nhi", [P, KT, T], F32R)
        nlo = sb("nlo", [P, KT, T], F32R)
        ident = sb("ident", [P, P])
        ones = sb("ones", [P, P])
        gmean = sb("gmean", [P, P])
        tri = sb("tri", [P, 1, P])
        eye8 = sb("eye8", [P, NB, NB])
        prm = sb("prm", [P, PEND])
        prmB = sb("prmB", [P, 4, 2 * RB])
        SA = sb("SA", [P, 2, 2 * NB * 30])
        c8 = sb("c8", [P, 2, 2, 2])
        m0 = sb("m0", [H, 2, NB])
        bg = sb("bg", [H, 2, 2])
        rstd = sb("rstd", [P, 1, T])
        rcol = sb("rcol", [P, 4])
        biases = sb("biases", [P, NE])
        wrt = sb("wrt", [P, KT, NE + 1])
        unit9 = sb("unit9", [P, NE + 1])
        row9 = sb("row9", [NE + 1, T])
        brt = sb("brt", [1, NE])
        iota = sb("iota", [P, P])
        before = sb("before", [P, P])
        startup = ExitStack()
        x_rows = sb("x_rows", [P, 3, D], where=startup)
        rowsA = sb("rowsA", [2 * RA, 256], where=startup)
        rowsB = sb("rowsB", [2 * RB, 512], where=startup)
        rowsC = sb("rowsC", [2 * RC, 256], where=startup)
        rowsN = sb("rowsN", [RN, D], where=startup)
        rowsSA = sb("rowsSA", [120, 4, 256], where=startup)
        rowsS = sb("rowsS", [2 * NB * H, P], where=startup)
        lam_t = sb("lam_t", [P, 6, 4], where=startup)
        startup.close()
        mix = ExitStack()
        qT = sb("qT", [P, H, T], where=mix)
        kT = sb("kT", [P, H, T], where=mix)
        vT = sb("vT", [P, H, T], where=mix)
        apad = sb("apad", [P, 2, 30 + T], where=mix)
        ac = sb("ac", [P, 2, T], where=mix)
        sga = sb("sga", [P, 2, T], where=mix)
        xbp = sb("xbp", [P, H, 3 + T], where=mix)
        cb = sb("cb", [P, H, T], where=mix)
        xcp = sb("xcp", [P, 2, 3 + T], where=mix)
        xcv = sb("xcv", [P, 2, T], where=mix)
        gg = sb("gg", [P, 2, T], where=mix)
        ra = sb("ra", [P, 2, T], where=mix)
        ix = sb("ix", [P, 2, T], where=mix)
        ktok = sb("ktok", [P, 3, H * P], where=mix)
        v1 = sb("v1", [P, 3, H, P + 1], where=mix)
        E = sb("E", [P, H, 384], where=mix)
        Cs = sb("Cs", [P, H, NB, P + 1], where=mix)
        Cp = sb("Cp", [P, H, P + 1], where=mix)
        rows = sb("rows", [H, 7, T], where=mix)
        cols = sb("cols", [P, 3, 3, H], where=mix)
        Qm = sb("Qm", [P, H, NB, NB], where=mix)
        dec = sb("dec", [P, H, 1, NB], where=mix)
        gsm = sb("gsm", [NB, H, NB], where=mix)
        vg = sb("vg", [P, 2, 2, P + 1], where=mix)
        gcol = sb("gcol", [P, H, 2], where=mix)
        gs = sb("gs", [NB, H], where=mix)
        st6 = sb("st6", [P, 3, H, 6], where=mix)
        mv = sb("mv", [P, 3, H, 2], where=mix)
        hr = sb("hr", [P, 3, H], where=mix)
        smp = sb("smp", [P, 440], where=mix)
        wq = sb("wq", [P, 3, H, P], where=mix)
        wg = sb("wg", [P, 12, 36], where=mix)
        wr = sb("wr", [P, 2, 2, P], where=mix)
        red = sb("red", [P, H, NB], where=mix)
        soh = sb("soh", [36, 384], where=mix)
        mix.close()
        ffn = ExitStack()
        n32 = sb("n32", [P, KT, T], where=ffn)
        hhi = sb("hhi", [P, 22, T], F32R, where=ffn)
        hlo = sb("hlo", [P, 22, T], F32R, where=ffn)
        sg = sb("sg", [P, 4, T], where=ffn)
        ffn.close()
        moe = ExitStack()
        sb("n32_below", [P, KT * T], where=moe)
        thi = sb("thi", [P, 3, D + 2 * NE], F32R, where=moe)
        tlo = sb("tlo", [P, 3, D], F32R, where=moe)
        sel = sb("sel", [P, 3, P], F32R, where=moe)
        selT = sb("selT", [P, T], F32R, where=moe)
        xe = sb("xe", [P, D], where=moe)
        ehi = sb("ehi", [P, KT, P], F32R, where=moe)
        elo = sb("elo", [P, KT, P], F32R, where=moe)
        sgm = sb("sgm", [P, PB], where=moe)
        hm = sb("hm", [P, 2, PB], where=moe)
        fhi = sb("fhi", [P, 2, 4, P], F32R, where=moe)
        flo = sb("flo", [P, 2, 4, P], F32R, where=moe)
        yhi = sb("yhi", [P, D], F32R, where=moe)
        ylo = sb("ylo", [P, D], F32R, where=moe)
        lg = sb("lg", [P, 3, NE], where=moe)
        top = sb("top", [P, 3, NE], where=moe)
        topi = sb("topi", [P, 3, NE], U32, where=moe)
        topf = sb("topf", [P, 3, 2], where=moe)
        oh = sb("oh", [P, 3, 2, NE], where=moe)
        gt = sb("gt", [P, 3, 4], where=moe)
        chosen = sb("chosen", [P, 3, NE + 1], where=moe)
        rank = sb("rank", [P, 3, NE + 1], where=moe)
        comb = sb("comb", [P, 3, NE], where=moe)
        geall = sb("geall", [P, NE + 1], where=moe)
        ge = sb("ge", [P, 2], where=moe)
        cnt = sb("cnt", [P, 4], where=moe)
        cnti = sb("cnti", [P, 1], I32, where=moe)
        moe.close()
        squares = ExitStack()
        sb("n32_below3", [P, KT * T], where=squares)
        sq = sb("sq", [P, KT, T], where=squares)
        squares.close()
        fin = ExitStack()
        sb("n32_below2", [P, KT * T], where=fin)
        yrow = sb("yrow", [P, 3, D], where=fin)
        fin.close()
        ps = ctx.enter_context(nc.psum_tensor("ps", [P, 8, PB], F32))

        raw_in = [sem(f"raw_in{i}") for i in range(NRAW)]
        hi_done, lo_done, lo_pool = sem("hi_done"), sem("lo_done"), sem("lo_pool")
        used = sem("unit_used")
        free = [sem("half0_free"), sem("half1_free")]
        S = {n: sem(n) for n in (
            "x_in", "gain_in", "prm_in", "const_done", "start_T", "start_act", "start_dve", "lam_exp", "lam_abs", "lam_done",
            "pool_step", "act_step", "dve_step",
            "norm_sq", "norm_ps", "norm_rt", "norm_y", "norm_hi", "norm_lo", "x_new",
            "pads", "copied", "mix_w", "ga_in", "sga_done", "apad_done", "gg_in", "gg_done", "sz_done",
            "cb_conv", "cb_done", "xcv_done", "conv_a_done", "conv_a_taps",
            "ri_ps", "ri_done", "rg_act", "rg_dve", "rg_sqrt", "rg_done",
            "lna_ps", "lna_xm", "lna_sq", "lna_rt", "lna_inv", "lna_done",
            "q_ps", "k_ps", "v_ps", "q_out", "k_out", "v_out", "g_ps", "gate_f", "gate_abs", "gate_ln", "rows_done",
            "kt_ps", "vt_ps", "ktok_done", "v1_done", "ct_dve", "em_done", "R_ps", "R_dve", "E_done", "dec_done",
            "s_ps", "P_done", "vg_done", "cp_ps", "cp_out", "num_ps", "num_read", "var_done", "sd_done", "h_norm", "hT_ps", "sk_done",
            "cs_in", "cs_n", "gsm_done", "Vm_done", "outer_ps", "cs_new", "cs_used", "cs_out", "Qm_done", "ns_done", "np_done",
            "y_f32", "yb_done", "y_hi", "y_lo", "so_ps", "so_out", "stored",
            "silu_done", "hhi_done", "hlo_done",
            "moe_const", "router_in", "lg_ps", "top_done", "gate_exp", "route_done", "rk_ps", "rounds", "tT_ps", "tT_hi", "tT_lo",
            "row_out", "col_ps", "col_done",
            "sel_done", "xe_ps", "xe_act", "ge_dve", "selT_done", "xeT_ps", "ehi_done", "elo_done", "mg_used", "sgm_done", "hm_done",
            "fT_ps", "fhi_done", "flo_done", "yhi_done", "ylo_done", "sc_ps", "x_add", "ranks_moved",
            "yr_act", "yr_dve",
        )}

        def A_(l, r, i):
            c = PA0 + i * 2 * RA + l * RA + r
            return prm[:, c:c + 1]

        def N_(k, r):
            c = PN0 + k * RN + r
            return prm[:, c:c + 1]

        def C_(l, r, i, n=1):
            c = PC0 + i * 2 * RC + l * RC + r
            return prm[:, c:c + n]

        def B_(l, r, i, n=1):
            c = l * RB + r
            return prmB[:, i, c:c + n]

        def unit(t, u, a_, b_):
            return t[:, u % t.shape[1], 0:a_ * b_].rearrange("p (k c) -> p k c", k=a_)

        def split_low(engine, u, part):
            return engine.tensor_tensor(low[:, u % NRAW, part], raw[:, u % NRAW, part], whi[:, u % NHI, part].bitcast(F32), ALU.subtract)

        def bank(b, w=PB, p=P):
            return ps[0:p, b, 0:w]

        srcs = {"w_in": a["w_in"], "w_out": a["w_out"], "w_gate": a["w_gate"], "w_up": a["w_up"], "w_down": a["w_down"]}
        sov = qT[:, :, :].rearrange("p h t -> p (h t)")

        def so_tile(k):
            _, p, _, w = SO[k]
            return (sov[0:p, [0, 256, 768][k]:[0, 256, 768][k] + w] if k < 3 else soh[0:p, 256 * (k - 3):256 * (k - 3) + w])

        def pool_taps(t):
            t = t[:, :, :, :] if len(t.shape) == 4 else t[:, :, :]
            names = "p a b c -> p (a b c)" if len(t.shape) == 4 else "p a b -> p (a b)"
            return t.rearrange(names)[:, 0:2 * TP].rearrange("p (i t) -> p i t", i=2)

        def token_rows(j, half, m):
            return bank((4 if half else 1) + j, PB, m)

        def rg_temp(k):
            return wq[:, :, :, :].rearrange("p a b c -> p (a b c)")[:, 2 * T * k:2 * T * (k + 1)].rearrange("p (i t) -> p i t", i=2)

        def value_rows(h):
            t = (kT, qT)[h % 2][0:NB, :, :].rearrange("p a b -> p (a b)")
            return t[:, 0:NB * (P + 1)]

        def outer_bank(h, j):
            return (0, 1, 2)[j] if h % 2 == 0 else (3, 6, 7)[j]

        block = ctx.enter_context(nc.Block())

        @block.sync
        def _(sp):
            def parameters():
                loads = [(rowsSA[:, :, :], a["state_conv_a"].rearrange("l (s b) k c -> (b k) (l s) c", s=2)),
                         (rowsS[:, :], a["state_mlstm_n"].rearrange("l b h k -> (l b h) k")),
                         (m0[:, :, :], a["state_mlstm_m"].rearrange("l b h -> h l b")),
                         (bg[:, :, 0:1], a["b_ig"].rearrange("l (h o) -> h l o", o=1)), (bg[:, :, 1:2], a["b_fg"].rearrange("l (h o) -> h l o", o=1))]
                for l in range(DEPTH):
                    def put(rows_, r, n, name, l=l):
                        src = a[name][l:l + 1] if n == 1 else a[name][l]
                        return rows_[r:r + n, :], src
                    r = l * RA
                    loads += [put(rowsA, r, CA, "conv_a_w"), put(rowsA, r + 31, 1, "conv_a_b"), put(rowsA, r + 32, 1, "ln_a_g"), put(rowsA, r + 33, 1, "ln_a_b")]
                    r = l * RB
                    loads += [put(rowsB, r, CB, "conv_b_w"), put(rowsB, r + 4, 1, "conv_b_b"), put(rowsB, r + 5, 1, "gn_b_g"), put(rowsB, r + 6, 1, "skip_b"),
                              (rowsB[r + 7:r + 31, :], a["state_conv_b"][l].rearrange("b k c -> (b k) c"))]
                    r = l * RC
                    loads += [put(rowsC, r, CC, "conv_c_w"), put(rowsC, r + 4, 1, "conv_c_b"), put(rowsC, r + 5, 1, "b_ra"), put(rowsC, r + 6, 1, "b_ix"),
                              put(rowsC, r + 7, 1, "lam"), (rowsC[r + 8:r + 16, :], a["state_rglru_h"][l]),
                              (rowsC[r + 16:r + 40, :], a["state_conv_c"][l].rearrange("b k c -> (b k) c"))]
                assert len(loads) == PRM_DMAS, len(loads)
                with nc.allow_non_contiguous_dma(reason="a few numbers, one to a partition"):
                    for dst, src in loads:
                        sp.dma_start(dst, src).then_inc(S["prm_in"], 16)

            def mixer_weights(l):
                sp.wait_ge(S["pads"], 6 * (l + 1))
                with nc.allow_non_contiguous_dma(reason="columns of the gates' weights"):
                    for g, n in enumerate(("w_ra", "w_ix")):
                        for q in range(2):
                            half = slice(64 * q, 64 * q + 64)
                            sp.dma_start(wr[half, g, :, half], a[n][l].rearrange("(i q) a b -> q a i b", q=2)[q]).then_inc(S["mix_w"], 16)
                    for j, n in enumerate(("w_q", "w_k", "w_v")):
                        sp.dma_start(wq[:, j, :, :], a[n][l].rearrange("h i j -> i h j")).then_inc(S["mix_w"], 16)
                    for o, n in ((0, "w_ig"), (32, "w_fg")):
                        sp.dma_start(wg[:, :, o:o + H], a[n][l].rearrange("(c p) h -> p c h", p=P)).then_inc(S["mix_w"], 16)

            for dst, src in ((rowsN[0:2, :], a["norm_mix_g"]), (rowsN[2:4, :], a["norm_ffn_g"]),
                             (rowsN[4:5, :], a["norm_final_g"].rearrange("(o c) -> o c", o=1))):
                sp.dma_start(dst, src).then_inc(S["gain_in"], 16)

            mixer_weights_before = {FIRST_UNIT[0] + 8: 0, FIRST_UNIT[20] + 6: 1}
            for u, (name, l, c0, w, ks) in enumerate(UNITS):
                if u == NRAW:
                    parameters()
                if u in mixer_weights_before:
                    mixer_weights(mixer_weights_before[u])
                if u >= NRAW:
                    sp.wait_ge(used, u - NRAW + 1)
                ll = l if name in ("w_in", "w_out") else 0
                kt = len(ks)
                dst = raw[:, u % NRAW, 0:kt * w].rearrange("p (k c) -> p k c", k=kt)
                for i, j in pieces(ks):
                    src = srcs[name][ll, ks[i] * P:(ks[j - 1] + 1) * P, c0:c0 + w].rearrange("(k p) c -> p k c", p=P)
                    sp.dma_start(dst[:, i:j, :], src).then_inc(raw_in[u % NRAW], 16)

            def stream(it, e):
                for c, (name, g, k0, kt, w) in enumerate(EU):
                    sp.wait_ge(used, it * NU + ND + c - NRAW + 1)
                    if name == "down":
                        src = a["we_down"][0, bass.ds(e, 1), k0 * P:(k0 + kt) * P, :]
                    else:
                        src = a["we_" + name][0, bass.ds(e, 1), k0 * P:(k0 + kt) * P, 512 * g:512 * g + w]
                    src = src.rearrange("o (k p) c -> p (o k) c", p=P)
                    dst = raw[:, c % NRAW, 0:kt * w].rearrange("p (k c) -> p k c", k=kt)
                    sp.dma_start(dst, src).then_inc(raw_in[c % NRAW], 16)

            stream(0, 0)
            with sp.Fori(1, NE) as e:
                stream(e, e)
            sp.wait_ge(S["rounds"], 1)
            nr = sp.value_load(cnti[0:1, 0:1], min_val=1, max_val=3)
            with sp.If(nr > 1):
                with sp.Fori(1, nr) as r:
                    with sp.Fori(0, NE) as e:
                        stream(r * NE + e, e)
            sp.wait_ge(S["yr_dve"], 2)
            sp.wait_ge(S["yr_act"], 1)
            yp = out["y_p"].rearrange("o (t p) c -> p (o t) c", p=P)
            sp.dma_start(yp, yrow[:, 0:2, :]).then_inc(S["x_in"], 16)
            sp.dma_start(out["y_s"].rearrange("b o c -> b (o c)"), yrow[0:NB, 2, :]).then_inc(S["x_in"], 16)
            sp.wait_ge(S["x_in"], 64)

        @block.tensor
        def _(pe):
            def startup_turns():
                pe.wait_ge(S["const_done"], 1)
                pe.wait_ge(S["x_in"], 32)
                for k in range(KT):
                    for j, (t0, n) in enumerate(TILES):
                        last = pe.transpose(ps[:, k, t0:t0 + n], x_rows[0:n, j, k * P:(k + 1) * P], ident[0:n, 0:n])
                    last.then_inc(S["start_T"], 1)
                pe.wait_ge(S["gain_in"], 48)
                pe.wait_ge(S["start_act"], 1)
                for k in range(KT):
                    last = pe.transpose(ps[:, 0, PN0 + k * RN:PN0 + (k + 1) * RN], rowsN[:, k * P:(k + 1) * P], ident[0:RN, 0:RN])
                last.then_inc(S["start_T"], 1)

            def parameter_turns():
                pe.wait_ge(S["prm_in"], 16 * PRM_DMAS)
                pe.wait_ge(S["norm_rt"], 1)
                for i in range(2):
                    pe.transpose(ps[:, 5, PA0 + i * 2 * RA:PA0 + (i + 1) * 2 * RA], rowsA[:, i * P:(i + 1) * P], ident[0:2 * RA, 0:2 * RA])
                for i in range(2):
                    pe.transpose(ps[:, 5, PC0 + i * 2 * RC:PC0 + (i + 1) * 2 * RC], rowsC[:, i * P:(i + 1) * P], ident[0:2 * RC, 0:2 * RC])
                pe.transpose(ps[:, 5, PS0:PEND], rowsS[:, :], ident[0:64, 0:64]).then_inc(S["start_T"], 1)
                for i in range(4):
                    last = pe.transpose(ps[:, 6, i * 2 * RB:(i + 1) * 2 * RB], rowsB[:, i * P:(i + 1) * P], ident[0:2 * RB, 0:2 * RB])
                last.then_inc(S["start_T"], 1)
                for i in range(2):
                    for j in range(4):
                        last = pe.transpose(ps[:, (4, 7)[i], j * 120:(j + 1) * 120], rowsSA[:, j, i * P:(i + 1) * P], ident[0:120, 0:120])
                last.then_inc(S["start_T"], 1)
                pe.wait_ge(S["start_act"], 5)
                pe.wait_ge(S["start_dve"], 2)

            def norm(n):
                pe.wait_ge(S["norm_sq"], n + 1)
                for k in range(KT):
                    last = pe.matmul(bank(4, T), ones[:, :], n32[:, k, :], start=(k == 0), stop=(k == KT - 1))
                last.then_inc(S["norm_ps"], 1)

            def token_norm(n, half):
                pe.wait_ge(S["norm_sq"], 3 + 2 * (n - 3) + half + 1)
                pe.wait_ge(S["norm_y"], 2 * (n - 3) + half + 1)
                if n == 3 and half == 0:
                    pe.wait_ge(S["router_in"], 32)
                if half == 0:
                    pe.wait_ge(S["moe_const"], 3)
                for k in range(4 * half, 4 * half + 4):
                    if n == 3:
                        pe.matmul(bank(0, T, NE + 1), wrt[:, k, :], n32[:, k, :], start=(k == 0), stop=False)
                    last = pe.matmul(bank(0, T, NE + 1), unit9[:, :], sq[:, k, :], start=(n == 4 and k == 0), stop=(k == KT - 1))
                if half:
                    last.then_inc(S["lg_ps"], 1)
                for j, (t0, m) in enumerate(TILES):
                    for k in range(4):
                        last = pe.transpose(ps[0:m, (4 if half else 1) + j, k * P:(k + 1) * P], n32[:, 4 * half + k, t0:t0 + m], ident[:, :])
                last.then_inc(S["tT_ps"], 1)
                if half:
                    pe.wait_ge(S["row_out"], n - 2)
                    if n == 3:
                        pe.matmul(ps[:, 0, BI0:BI0 + NE], ones[0:1, :], brt[:, :], start=True, stop=True)
                    for j, (t0, m) in enumerate(TILES):
                        c = LG0 + j * (NE + 1)
                        last = pe.transpose(ps[0:m, 0, c:c + NE + 1], row9[:, t0:t0 + m], ident[0:NE + 1, 0:NE + 1])
                    last.then_inc(S["col_ps"], 1)

            def split_ready(u):
                pe.wait_ge(hi_done, u + 1)
                pe.wait_ge(lo_done, u + 1)
                if u in POOL_UNITS:
                    pe.wait_ge(lo_pool, POOL_UNITS.index(u) + 1)

            def group(G, xhi, xlo, units=None):
                _, l, c0, w, ks = GROUPS[G]
                n = {0: 0, 6: 1, 20: 2}.get(G)
                before_it = {1: 0, 7: 1, 21: 2}.get(G)
                if before_it is not None:
                    pe.wait_ge(S["norm_rt"], before_it + 1)
                if G // 2 > 0:
                    pe.wait_ge(free[G % 2], G // 2)
                for j in range(len(ks)) if units is None else units:
                    u = FIRST_UNIT[G] + j
                    if n is not None:
                        pe.wait_ge(S["norm_hi"], 2 * n + j + 1)
                        pe.wait_ge(S["norm_lo"], 2 * n + j + 1)
                    split_ready(u)
                    hi, lo = unit(whi, u, len(ks[j]), w), unit(low, u, len(ks[j]), w)
                    for i in range(w // P):
                        o = bank(4 * (G % 2) + i, T)
                        for k, kx in enumerate(ks[j]):
                            c = slice(i * P, (i + 1) * P)
                            first, end = (j, k) == (0, 0), (j, k) == (len(ks) - 1, len(ks[j]) - 1)
                            pe.matmul(o, hi[:, k, c], xhi[:, kx, :], start=first, stop=False)
                            pe.matmul(o, hi[:, k, c], xlo[:, kx, :], start=False, stop=False)
                            last = pe.matmul(o, lo[:, k, c], xhi[:, kx, :], start=False, stop=end)
                    last.then_inc(used, 1)
                    if n is not None and j == 0:
                        if G > 0:
                            pe.wait_ge(free[1], G // 2)
                        norm(n)

            def mixer_products(l):
                pe.wait_ge(S["mix_w"], 16 * MIX_DMAS * (l + 1))
                pe.wait_ge(S["cb_done"], l + 1)
                pe.wait_ge(free[1], HALF1[l])
                for h in range(H):
                    last = pe.matmul(bank(4 + h, T), wq[:, 0, h, :], cb[:, h, :], start=True, stop=True)
                last.then_inc(S["q_ps"], 1)
                pe.wait_ge(free[0], HALF0[l])
                for h in range(H):
                    last = pe.matmul(bank(h, T), wq[:, 1, h, :], cb[:, h, :], start=True, stop=True)
                last.then_inc(S["k_ps"], 1)
                pe.wait_ge(S["q_out"], l + 1)
                pe.wait_ge(S["xcv_done"], l + 1)
                for g in range(2):
                    for i in range(2):
                        last = pe.matmul(bank(4 + 2 * g + i, T), wr[:, g, i, :], xcv[:, i, :], start=True, stop=True)
                last.then_inc(S["ri_ps"], 1)
                pe.wait_ge(S["k_out"], l + 1)
                for h in range(H):
                    last = pe.matmul(bank(h, T), wq[:, 2, h, :], xbp[:, h, 3:3 + T], start=True, stop=True)
                last.then_inc(S["v_ps"], 1)

            def mixer_gates(l):
                pe.wait_ge(S["ri_done"], 4 * (l + 1))
                pe.wait_ge(S["v_out"], l + 1)
                for h in range(H):
                    for j, t in enumerate((qT, kT, vT)):
                        c = 3 * h + j
                        last = pe.matmul(bank(4, T, 36), wg[:, c, :], t[:, h, :], start=(c == 0), stop=(c == 11))
                last.then_inc(S["g_ps"], 1)

            def mixer_keys_turned(l):
                for j, (t0, n) in enumerate(TILES):
                    for h in range(H):
                        last = pe.transpose(ps[0:n, j, h * P:(h + 1) * P], kT[:, h, t0:t0 + n], ident[:, :])
                last.then_inc(S["kt_ps"], 1)

            def mixer_values_turned(l):
                pe.wait_ge(S["ktok_done"], 3 * (l + 1))
                for j, (t0, n) in enumerate(TILES):
                    for h in range(H):
                        last = pe.transpose(ps[0:n, j, h * P:(h + 1) * P], vT[:, h, t0:t0 + n], ident[:, :])
                last.then_inc(S["vt_ps"], 1)

            def mixer_broadcast(l):
                pe.wait_ge(S["v1_done"], 3 * (l + 1))
                pe.wait_ge(S["rows_done"], l + 1)
                for h in range(H):
                    pe.matmul(bank(h, T), ident[0:H, h:h + 1].to_broadcast([H, P]), rows[:, 4, :], start=True, stop=True)
                for j, (t0, n) in enumerate(TILES):
                    for r, row in enumerate((5, 3)):
                        c = COLS0 + (2 * j + r) * H
                        last = pe.transpose(ps[0:n, 3, c:c + H], rows[:, row, t0:t0 + n], ident[0:H, 0:H])
                last.then_inc(S["R_ps"], 1)

            def lna(l, step):
                if step == 0:
                    pe.wait_ge(S["conv_a_done"], 2 * (l + 1))
                else:
                    pe.wait_ge(S["lna_sq"], l + 1)
                if step == 0:
                    pe.wait_ge(free[1], 2 + 10 * l)
                for i in range(2):
                    last = pe.matmul(bank(5 + i, T), gmean[:, :], (ac if step == 0 else sga)[:, i, :], start=True, stop=True)
                last.then_inc(S["lna_ps"], 1)

            def mixer_scores(l, heads_):
                if heads_[0] == 0:
                    pe.wait_ge(S["E_done"], l + 1)
                    pe.wait_ge(S["dec_done"], l + 1)
                for h in heads_:
                    pe.matmul(ps[:, h, 0:TP], kT[:, h, 0:P], qT[:, h, 0:TP], start=True, stop=True)
                    pe.matmul(ps[:, h, TP:384], kT[:, h, P:TP], qT[:, h, P:TP], start=True, stop=True).then_inc(S["s_ps"], 1)

            def mixer_numerator(l):
                pe.wait_ge(S["lna_rt"], l + 1)
                pe.wait_ge(S["P_done"], l + 1)
                for h in range(H):
                    o = slice((h % 2) * (P + 1), (h % 2 + 1) * (P + 1))
                    pe.matmul(ps[:, 4 + h // 2, o], E[:, h, 0:P], v1[:, 0, h, :], start=True, stop=True)
                for h in range(H):
                    o = slice((h % 2) * (P + 1), (h % 2 + 1) * (P + 1))
                    pe.matmul(ps[:, 6 + h // 2, o], E[:, h, P:TP], v1[:, 0, h, :], start=True, stop=False)
                    last = pe.matmul(ps[:, 6 + h // 2, o], E[:, h, TP:384], v1[:, 1, h, :], start=False, stop=True)
                last.then_inc(S["num_ps"], 1)

            def mixer_prompt_state(l):
                for h in range(H):
                    pe.wait_ge(S["vg_done"], 4 * l + h + 1)
                    pe.matmul(ps[:, h, 0:P + 1], ktok[:, 0, h * P:(h + 1) * P], vg[:, h % 2, 0, :], start=True, stop=False)
                    pe.matmul(ps[:, h, 0:P + 1], ktok[:, 1, h * P:(h + 1) * P], vg[:, h % 2, 1, :], start=False, stop=True).then_inc(S["cp_ps"], 1)

            def mixer_samples(l):
                def outer(h):
                    n = 4 * l + h
                    pe.wait_ge(S["Vm_done"], n + 1)
                    if h >= 2:
                        pe.wait_ge(S["cs_new"], n - 1)
                    elif h == 1:
                        pe.wait_ge(S["num_read"], 2 * l + 1)
                    for j in range(3):
                        w = (3 if j < 2 else 2) * (P + 1)
                        last = pe.matmul(ps[:, outer_bank(h, j), 0:w], ktok[0:NB, 2, h * P:(h + 1) * P],
                                         value_rows(h)[:, 3 * j * (P + 1):3 * j * (P + 1) + w], start=True, stop=True)
                    last.then_inc(S["outer_ps"], 1)

                def query(h):
                    n = 4 * l + h
                    pe.wait_ge(S["cs_new"], n + 1)
                    o = slice((h % 2) * (P + 1), (h % 2 + 1) * (P + 1))
                    for b in range(NB):
                        last = pe.matmul(ps[0:NB, 4 + h // 2, o], Qm[:, h, b, :], Cs[:, h, b, :], start=(b == 0), stop=(b == NB - 1))
                    last.then_inc(S["cs_used"], 1)

                pe.wait_ge(S["cp_out"], l + 1)
                pe.wait_ge(S["Qm_done"], 4 * (l + 1))
                outer(0)
                outer(1)
                for h in range(H):
                    query(h)
                    if h + 2 < H:
                        outer(h + 2)

            def mixer_turn_back(l):
                pe.wait_ge(S["h_norm"], l + 1)
                ht = E[:, :, :].rearrange("p a b -> p (a b)").rearrange("p (t c) -> p t c", t=3)
                for h in range(H):
                    for j, (t0, n) in enumerate(TILES):
                        last = pe.transpose(ps[:, 4 + h, t0:t0 + n], ht[0:n, j, h * P:(h + 1) * P], ident[0:n, 0:n])
                last.then_inc(S["hT_ps"], 1)

            def mixer_state_rows(l):
                pe.wait_ge(S["rg_done"], l + 1)
                pe.wait_ge(S["ns_done"], l + 1)
                pe.wait_ge(S["np_done"], l + 1)
                pe.wait_ge(S["yb_done"], l + 1)
                pe.transpose(ps[0:36, 4, 256:384], smp[:, 400:436], ident[:, :])
                for i in range(2):
                    last = pe.transpose(ps[0:38, 4, i * P:(i + 1) * P], apad[:, i, 256:294], ident[:, :])
                last.then_inc(S["so_ps"], 1)
                for i in range(H):
                    last = pe.transpose(ps[0:11, 5, i * P:(i + 1) * P], xbp[:, i, 256:267], ident[:, :])
                last.then_inc(S["so_ps"], 1)
                for i in range(2):
                    last = pe.transpose(ps[0:11, 6, i * P:(i + 1) * P], xcp[:, i, 256:267], ident[:, :])
                last.then_inc(S["so_ps"], 1)
                for i in range(2):
                    last = pe.transpose(ps[0:9, 7, i * P:(i + 1) * P], xcv[:, i, 255:264], ident[:, :])
                last.then_inc(S["so_ps"], 1)

            def mixers(l):
                mixer_products(l)
                mixer_gates(l)
                mixer_keys_turned(l)
                pe.wait_ge(S["gate_f"], 2 * (l + 1))
                group(20 * l + 3, nhi, nlo, (0,))
                mixer_values_turned(l)
                mixer_broadcast(l)
                group(20 * l + 3, nhi, nlo, (1,))
                mixer_scores(l, (0, 1))
                lna(l, 0)
                mixer_scores(l, (2, 3))
                lna(l, 1)
                mixer_numerator(l)
                mixer_prompt_state(l)
                mixer_samples(l)
                pe.wait_ge(S["y_hi"], 3 * l + 2)
                pe.wait_ge(S["y_lo"], 3 * l + 2)
                group(20 * l + 4, nhi, nlo, (0,))
                mixer_turn_back(l)
                mixer_state_rows(l)

            startup_turns()
            pe.wait_ge(S["start_act"], 2)
            pe.wait_ge(S["start_dve"], 1)
            pe.wait_ge(S["const_done"], 2)
            for l in range(DEPTH):
                for g in range(3):
                    group(20 * l + g, nhi, nlo)
                    if l == 0 and g == 0:
                        parameter_turns()
                mixers(l)
                pe.wait_ge(S["y_hi"], 3 * (l + 1))
                pe.wait_ge(S["y_lo"], 3 * (l + 1))
                group(20 * l + 4, nhi, nlo, (1,))
                pe.wait_ge(S["so_out"], 5 * (l + 1))
                group(20 * l + 5, nhi, nlo)
                if l == 1:
                    token_norm(3, 0)
                if l == 0:
                    for g in range(12):
                        group(6 + g, nhi, nlo)
                    pe.wait_ge(S["hhi_done"], 5)
                    pe.wait_ge(S["hlo_done"], 5)
                    group(18, hhi, hlo, range(5))
                    pe.wait_ge(S["hhi_done"], 6)
                    pe.wait_ge(S["hlo_done"], 6)
                    group(18, hhi, hlo, (5,))
                    group(19, hhi, hlo)

            token_norm(3, 1)
            pe.wait_ge(S["route_done"], 1)
            for j, (t0, n) in enumerate(TILES + [(T, P)]):
                for i, (_, m) in enumerate(TILES[:j + 1]):
                    w = (before if i == j else ones)[0:m, 0:n]
                    last = pe.matmul(ps[0:n, 0, j * NE:(j + 1) * NE], w, chosen[0:m, i, 0:NE], start=(i == 0), stop=(i == min(j, 2)))
            last.then_inc(S["rk_ps"], 1)
            pe.wait_ge(S["tT_hi"], 7)
            pe.wait_ge(S["tT_lo"], 6)

            def gather(it):
                pe.wait_ge(S["sel_done"], it * 3 + 3)
                for half in range(2):
                    c = slice(half * PB, (half + 1) * PB)
                    for j, (_, n) in enumerate(TILES):
                        pe.matmul(bank(6 + half), sel[0:n, j, :], thi[0:n, j, c], start=(j == 0), stop=False)
                        last = pe.matmul(bank(6 + half), sel[0:n, j, :], tlo[0:n, j, c], start=False, stop=(j == 2))
                last.then_inc(S["xe_ps"], 1)

            def gather_turn(it):
                pe.wait_ge(S["xe_act"], it + 1)
                for k in range(KT):
                    last = pe.transpose(ps[:, 6 + k // 4, (k % 4) * P:(k % 4 + 1) * P], xe[:, k * P:(k + 1) * P], ident[:, :])
                last.then_inc(S["xeT_ps"], 1)

            def expert(it):
                def ready(c):
                    pe.wait_ge(hi_done, it * NU + ND + c + 1)
                    pe.wait_ge(lo_done, it * NU + ND + c + 1)
                    pe.wait_ge(lo_pool, it * NU + len(POOL_UNITS) + c + 1)

                def into_hidden(c, b):
                    _, g, k0, kt, w = EU[c]
                    ready(c)
                    hi, lo = unit(whi, c, kt, w), unit(low, c, kt, w)
                    for k in range(kt):
                        pe.matmul(bank(b, w), ehi[:, k0 + k, :], hi[:, k, :], start=(k0 + k == 0), stop=False)
                        pe.matmul(bank(b, w), ehi[:, k0 + k, :], lo[:, k, :], start=False, stop=False)
                        last = pe.matmul(bank(b, w), elo[:, k0 + k, :], hi[:, k, :], start=False, stop=(k0 + k == KT - 1))
                    last.then_inc(used, 1)

                def down(c):
                    _, g, k0, kt, w = EU[c]
                    ready(c)
                    hi, lo = unit(whi, c, kt, w), unit(low, c, kt, w)
                    for k in range(kt):
                        t = k0 + k
                        for half in range(2):
                            s = slice(half * PB, (half + 1) * PB)
                            fh, fl = fhi[:, g % 2, t - 4 * g, :], flo[:, g % 2, t - 4 * g, :]
                            pe.matmul(bank(4 + half), fh, hi[:, k, s], start=(t == 0), stop=False)
                            pe.matmul(bank(4 + half), fh, lo[:, k, s], start=False, stop=False)
                            last = pe.matmul(bank(4 + half), fl, hi[:, k, s], start=False, stop=(t == 10))
                    last.then_inc(used, 1)

                def turn_hidden(g, b):
                    pe.wait_ge(S["hm_done"], it * 3 + g + 1)
                    for i in range(FGW[g] // P):
                        last = pe.transpose(ps[:, b, i * P:(i + 1) * P], hm[:, g % 2, i * P:(i + 1) * P], ident[:, :])
                    last.then_inc(S["fT_ps"], 1)

                first = isinstance(it, int) and it == 0
                pe.wait_ge(S["ehi_done"], it + 1)
                pe.wait_ge(S["elo_done"], it + 1)
                if not first:
                    pe.wait_ge(S["hm_done"], it * 3)
                into_hidden(0, 0)
                into_hidden(1, 0)
                scatter(it, 0)
                into_hidden(2, 1)
                scatter(it, 1)
                into_hidden(3, 1)
                scatter(it, 2)
                if not first:
                    pe.wait_ge(S["flo_done"], it * 3)
                into_hidden(4, 2)
                scatter(it, 3)
                into_hidden(5, 2)
                pe.wait_ge(S["x_add"], it * 4 + 4)
                turn_hidden(0, 6)
                into_hidden(6, 3)
                for j, (t0, n) in enumerate(TILES):
                    pe.transpose(ps[:, 7, t0:t0 + n], sel[0:n, j, :].bitcast(F32), ident[0:n, 0:n])
                for j, (_, n) in enumerate(TILES):
                    for i in range(2):
                        last = pe.matmul(ps[:, 7, 272:272 + NE], sel[0:n, j, :], thi[0:n, j, D + i * NE:D + (i + 1) * NE],
                                         start=(j == 0 and i == 0), stop=(j == 2 and i == 1))
                last.then_inc(S["mg_used"], 1)
                into_hidden(7, 3)
                pe.wait_ge(S["fhi_done"], it * 3 + 1)
                pe.wait_ge(S["flo_done"], it * 3 + 1)
                down(8)
                down(9)
                pe.wait_ge(S["hm_done"], it * 3 + 1)
                into_hidden(10, 0)
                into_hidden(11, 0)
                pe.wait_ge(S["ge_dve"], it + 1)
                turn_hidden(1, 7)
                into_hidden(12, 1)
                into_hidden(13, 1)
                pe.wait_ge(S["fhi_done"], it * 3 + 2)
                pe.wait_ge(S["flo_done"], it * 3 + 2)
                down(14)
                down(15)
                turn_hidden(2, 2)
                gather(it + 1)
                pe.wait_ge(S["fhi_done"], it * 3 + 3)
                pe.wait_ge(S["flo_done"], it * 3 + 3)
                down(16)
                gather_turn(it + 1)
                down(17)

            def scatter(it, pair):
                if pair == 0:
                    pe.wait_ge(S["yhi_done"], it + 1)
                    pe.wait_ge(S["ylo_done"], it + 1)
                    pe.wait_ge(S["selT_done"], it + 1)
                else:
                    pe.wait_ge(S["x_add"], it * 4 + pair)
                for i in range(2):
                    c = slice((2 * pair + i) * P, (2 * pair + i + 1) * P)
                    pe.matmul(bank(6 + i, T), yhi[:, c], selT[:, :], start=True, stop=False)
                    last = pe.matmul(bank(6 + i, T), ylo[:, c], selT[:, :], start=False, stop=True)
                last.then_inc(S["sc_ps"], 1)

            gather(0)
            gather_turn(0)
            expert(0)
            with pe.Fori(1, NE) as e:
                expert(e)
            pe.wait_ge(S["rounds"], 1)
            nr = pe.value_load(cnti[0:1, 0:1], min_val=1, max_val=3)
            with pe.If(nr > 1):
                with pe.Fori(1, nr) as r:
                    with pe.Fori(0, NE) as e:
                        expert(r * NE + e)
                for pair in range(4):
                    scatter(nr * NE, pair)
            with pe.Else():
                for pair in range(4):
                    scatter(NE, pair)

            token_norm(4, 0)
            token_norm(4, 1)

        @block.scalar
        def _(act):
            steps = [0]

            def step(ins):
                steps[0] += 1
                ins.then_inc(S["act_step"], 1)

            def settle():
                act.wait_ge(S["act_step"], steps[0])

            act.dma_start(x_rows[:, 0:2, :], a["x_prompt"].rearrange("o (t p) c -> p (o t) c", p=P)).then_inc(S["x_in"], 16)
            act.dma_start(x_rows[0:NB, 2, :], a["x_sample"].rearrange("b o c -> b (o c)")).then_inc(S["x_in"], 16)

            def hi(u):
                n = UNITS[u][3] * len(UNITS[u][4])
                act.wait_ge(raw_in[u % NRAW], landed(u))
                if u >= NHI:
                    act.wait_ge(used, u - NHI + 1)
                act.activation(whi[:, u % NHI, 0:n], raw[:, u % NRAW, 0:n], ACT.Copy).then_inc(hi_done, 1)

            def norm_high(n, half):
                if n > 0:
                    act.wait_ge(free[half], TAKEN[n])
                    act.wait_ge(used, FIRST_UNIT[(0, 6, 18)[n]])
                for k in range(4 * half, 4 * half + 4):
                    last = act.activation(nhi[:, k, :], xT[:, k, :], ACT.Copy, scale=N_(k, NORM_ROW[n]))
                last.then_inc(S["norm_hi"], 1)

            def norm_square(n):
                if n == 1:
                    act.wait_ge(S["stored"], 16 * STORES)
                act.activation(n32[:, :, :], xT[:, :, :], ACT.Square).then_inc(S["norm_sq"], 1)

            def norm_root(n):
                act.wait_ge(S["norm_ps"], n + 1)
                act.activation(rstd[:, 0, :], bank(4, T), ACT.Sqrt, scale=1.0 / D, bias=EPS).then_inc(S["norm_rt"], 1)

            def token_norm(n):
                if n == 4:
                    act.wait_ge(S["x_new"], 1)
                else:
                    act.wait_ge(S["stored"], 16 * STORES * DEPTH)
                for half in range(2):
                    if n == 3:
                        act.wait_ge(free[half], TAKEN[n])
                    c = slice(4 * half, 4 * half + 4)
                    act.activation(sq[:, c, :], xT[:, c, :], ACT.Square).then_inc(S["norm_sq"], 1)
                act.wait_ge(S["lg_ps"], n - 2)
                act.activation(row9[:, :], bank(0, T, NE + 1), ACT.Copy).then_inc(S["row_out"], 1)
                act.wait_ge(S["col_ps"], n - 2)
                act.activation(rcol[:, 0:2], ps[:, 0, LG0 + NE:LG0 + 2 * NE + 2:NE + 1], ACT.Sqrt, scale=1.0 / D, bias=EPS).then_inc(S["norm_rt"], 1)
                c = LG0 + 3 * NE + 2
                act.activation(rcol[0:NB, 2:3], ps[0:NB, 0, c:c + 1], ACT.Sqrt, scale=1.0 / D, bias=EPS).then_inc(S["norm_rt"], 1)

            act.wait_ge(S["start_T"], 4)
            act.activation(xT[:, 0:4, :], ps[:, 0:4, 0:T], ACT.Copy).then_inc(S["start_act"], 1)
            act.wait_ge(S["start_T"], 9)
            act.activation(prm[:, PN0:PC0], ps[:, 0, PN0:PC0], ACT.Copy).then_inc(S["start_act"], 1)

            def parameters_out():
                act.wait_ge(S["start_T"], 10)
                act.activation(prm[:, 0:PN0], bank(5, PN0), ACT.Copy).then_inc(S["start_act"], 1)
                act.activation(prm[:, PC0:PEND], ps[:, 5, PC0:PEND], ACT.Copy).then_inc(S["start_act"], 1)
                act.wait_ge(S["start_T"], 12)
                act.activation(SA[:, 0, :], bank(4, 480), ACT.Copy)
                act.activation(SA[:, 1, :], bank(7, 480), ACT.Copy).then_inc(S["start_act"], 1)
                act.wait_ge(S["lam_abs"], 1)
                act.activation(lam_t[:, 1, :], lam_t[:, 0, :], ACT.Exp, scale=-1.0).then_inc(S["lam_exp"], 1)

            def layer(l):
                U = FIRST_UNIT[20 * l]
                if l == 0:
                    act.wait_ge(S["start_act"], 2)
                norm_high(2 * l, 0)
                hi(U)
                if l == 0:
                    act.wait_ge(S["start_dve"], 1)
                    norm_high(0, 1)
                    hi(U + 1)
                else:
                    hi(U + 1)
                    norm_high(2, 1)
                norm_square(2 * l)
                hi(U + 2)
                norm_root(2 * l)
                hi(U + 3)
                if l == 0:
                    parameters_out()
                act.wait_ge(S["ga_in"], l + 1)
                act.activation(sga[:, :, :], sga[:, :, :], ACT.Sigmoid).then_inc(S["sga_done"], 1)
                hi(U + 4)
                hi(U + 5)
                act.wait_ge(S["cb_conv"], l + 1)
                act.activation(cb[:, :, :], cb[:, :, :], ACT.Silu).then_inc(S["cb_done"], 1)
                hi(U + 6)
                act.wait_ge(S["gg_in"], l + 1)
                act.activation(gg[:, :, :], gg[:, :, :], ACT.Gelu_apprx_tanh).then_inc(S["gg_done"], 1)
                act.wait_ge(S["q_ps"], l + 1)
                act.activation(qT[:, :, :], ps[:, 4:8, 0:T], ACT.Copy).then_inc(S["q_out"], 1)
                act.wait_ge(S["k_ps"], l + 1)
                act.activation(kT[:, :, :], ps[:, 0:4, 0:T], ACT.Copy, scale=float(P) ** -0.5).then_inc(S["k_out"], 1)
                act.wait_ge(S["ri_ps"], l + 1)
                for i in range(2):
                    act.activation(ra[:, i, :], bank(4 + i, T), ACT.Sigmoid, bias=C_(l, 5, i)).then_inc(S["ri_done"], 1)
                for i in range(2):
                    act.activation(ix[:, i, :], bank(6 + i, T), ACT.Sigmoid, bias=C_(l, 6, i)).then_inc(S["ri_done"], 1)
                act.wait_ge(S["v_ps"], l + 1)
                act.activation(vT[:, :, :], ps[:, 0:4, 0:T], ACT.Copy).then_inc(S["v_out"], 1)
                hi(U + 7)
                act.wait_ge(S["g_ps"], l + 1)
                act.activation(rows[:, 0, :], ps[0:H, 4, 0:T], ACT.Identity, bias=bg[:, l, 0:1]).then_inc(S["gate_f"], 1)
                act.activation(rows[:, 1, :], ps[32:32 + H, 4, 0:T], ACT.Identity, bias=bg[:, l, 1:2]).then_inc(S["gate_f"], 1)
                act.wait_ge(S["kt_ps"], l + 1)
                for j, (_, n) in enumerate(TILES):
                    act.activation(ktok[0:n, j, :], ps[0:n, j, :], ACT.Copy).then_inc(S["ktok_done"], 1)
                act.wait_ge(S["gate_abs"], l + 1)
                step(act.activation(rows[:, 2, :], rows[:, 2, :], ACT.Exp, scale=-1.0))
                settle()
                act.activation(rows[:, 2, :], rows[:, 2, :], ACT.Ln, bias=1.0).then_inc(S["gate_ln"], 1)
                act.wait_ge(S["vt_ps"], l + 1)
                for j, (_, n) in enumerate(TILES):
                    act.activation(v1[0:n, j, :, 0:P], ps[0:n, j, :].rearrange("p (h c) -> p h c", h=H), ACT.Copy).then_inc(S["v1_done"], 1)
                act.wait_ge(S["ri_done"], 4 * (l + 1))
                tmp = rg_temp(0)
                for i in range(2):
                    act.activation(tmp[:, i, :], ra[:, i, :], ACT.Tanh, scale=c8[:, 1, i, l:l + 1]).then_inc(S["rg_act"], 1)
                act.wait_ge(S["rg_act"], 4 * l + 2)
                for i in range(2):
                    act.activation(ra[:, i, :], ra[:, i, :], ACT.Exp, scale=c8[:, 0, i, l:l + 1]).then_inc(S["rg_act"], 1)
                act.wait_ge(S["ct_dve"], 2 * (l + 1))
                act.activation(cols[:, 0:2, 2, :], cols[:, 0:2, 1, :], ACT.Exp, scale=-1.0).then_inc(S["em_done"], 1)
                act.activation(cols[0:NB, 2, 2, :], cols[0:NB, 2, 1, :], ACT.Exp, scale=-1.0).then_inc(S["em_done"], 1)
                act.activation(gs[:, :], cols[0:NB, 2, 0, :], ACT.Exp).then_inc(S["em_done"], 1)
                act.wait_ge(S["R_dve"], 3 * (l + 1))
                act.activation(dec[:, :, 0, :], ps[:, 0:4, TP:T], ACT.Exp).then_inc(S["dec_done"], 1)
                for h in range(H):
                    act.activation(E[:, h, 0:TP], E[:, h, 0:TP], ACT.Exp, bias=cols[:, 0, 0, h:h + 1])
                    last = act.activation(E[:, h, TP:384], E[:, h, TP:384], ACT.Exp, bias=cols[:, 1, 0, h:h + 1])
                last.then_inc(S["E_done"], 1)
                act.wait_ge(S["rg_dve"], l + 1)
                act.activation(tmp, tmp, ACT.Sqrt).then_inc(S["rg_sqrt"], 1)
                hi(U + 8)
                act.wait_ge(free[1], 2 + 10 * l)
                act.activation(vT[:, :, :], vT[:, :, :], ACT.Sigmoid).then_inc(S["sz_done"], 1)
                act.wait_ge(S["lna_xm"], l + 1)
                act.activation(sga[:, :, :], ac[:, :, :], ACT.Square).then_inc(S["lna_sq"], 1)
                act.wait_ge(S["lna_ps"], 2 * (l + 1))
                act.activation(sga[:, :, :], ps[:, 5:7, 0:T], ACT.Sqrt, bias=LN_EPS).then_inc(S["lna_rt"], 1)
                hi(U + 9)
                act.wait_ge(S["cp_ps"], 4 * (l + 1))
                act.activation(Cp[:, :, :], ps[:, 0:4, 0:P + 1], ACT.Copy).then_inc(S["cp_out"], 1)
                act.wait_ge(S["cp_out"], l + 1)
                act.activation(smp[:, 432:436], Cp[:, :, P], ACT.Copy).then_inc(S["np_done"], 1)
                hi(U + 10)
                act.wait_ge(S["lna_done"], l + 1)
                for i in range(2):
                    last = act.activation(ac[:, i, :], ac[:, i, :], ACT.Silu, scale=A_(l, 32, i), bias=A_(l, 33, i))
                last.then_inc(S["y_f32"], 1)
                act.wait_ge(S["y_f32"], l + 1)
                act.activation(nhi[:, 0:2, :], ac[:, :, :], ACT.Copy).then_inc(S["y_hi"], 1)
                act.wait_ge(S["var_done"], 2 * l + 1)
                act.activation(hr[:, 0:2, :], mv[:, 0:2, :, 1], ACT.Sqrt, bias=LN_EPS).then_inc(S["sd_done"], 1)
                act.wait_ge(S["rg_done"], l + 1)
                act.activation(nhi[:, 6:8, :], gg[:, :, :], ACT.Copy).then_inc(S["y_hi"], 1)
                for h in range(H):
                    last = act.activation(cb[:, h, :], cb[:, h, :], ACT.Copy, scale=B_(l, 6, h))
                last.then_inc(S["sk_done"], 1)
                act.wait_ge(S["var_done"], 2 * l + 2)
                act.activation(hr[0:NB, 2, :], mv[0:NB, 2, :, 1], ACT.Sqrt, bias=LN_EPS).then_inc(S["sd_done"], 1)
                act.wait_ge(S["yb_done"], l + 1)
                act.activation(nhi[:, 2:6, :], cb[:, :, :], ACT.Copy).then_inc(S["y_hi"], 1)
                for k, (b, p, c0, w) in enumerate(SO):
                    act.wait_ge(S["so_ps"], 4 * l + min(k + 1, 4))
                    act.activation(so_tile(k), ps[0:p, b, c0:c0 + w], ACT.Copy).then_inc(S["so_out"], 1)
                hi(U + 11)

            layer(0)
            hi(12)
            hi(13)
            norm_high(1, 0)
            norm_high(1, 1)
            norm_square(1)
            hi(14)
            norm_root(1)
            for g in range(6):
                u, n = 12 + 4 * g, GROUPS[6 + 2 * g][3] // P
                hi(u + 3)
                hi(u + 4)
                act.wait_ge(free[0], 4 + g)
                act.activation(sg[:, 0:n, :], sg[:, 0:n, :], ACT.Silu).then_inc(S["silu_done"], 1)
                hi(u + 5)
                hi(u + 6)
                act.wait_ge(free[1], 4 + g)
                act.activation(hhi[:, 4 * g:4 * g + n, :], sg[:, 0:n, :], ACT.Copy).then_inc(S["hhi_done"], 1)
            for u in range(39, 48):
                hi(u)
            layer(1)
            token_norm(3)

            for j, (_, n) in enumerate(TILES):
                act.wait_ge(S["top_done"], j + 1)
                act.activation(gt[0:n, j, 1:2], gt[0:n, j, 0:1], ACT.Exp).then_inc(S["gate_exp"], 1)
            for j, (_, n) in enumerate(TILES):
                if j == 0:
                    act.wait_ge(S["tT_ps"], 2)
                    act.wait_ge(S["col_done"], 2)
                for half in range(2):
                    c = slice(half * PB, (half + 1) * PB)
                    act.activation(thi[0:n, j, c], token_rows(j, half, n), ACT.Copy, scale=rcol[0:n, j:j + 1]).then_inc(S["tT_hi"], 1)
            act.wait_ge(S["route_done"], 1)
            for j, (_, n) in enumerate(TILES):
                last = act.activation(thi[0:n, j, D:D + NE], comb[0:n, j, :], ACT.Copy)
            last.then_inc(S["tT_hi"], 1)

            def take_rows(it):
                act.wait_ge(S["xe_ps"], it + 1)
                act.activation(xe[:, :], ps[:, 6:8, :].rearrange("p b c -> p (b c)"), ACT.Copy).then_inc(S["xe_act"], 1)

            def take_turned(it):
                act.wait_ge(S["xeT_ps"], it + 1)
                act.activation(ehi[:, :, :], ps[:, 6:8, :].rearrange("p b (k c) -> p (b k) c", k=4), ACT.Copy).then_inc(S["ehi_done"], 1)

            def y_high(it):
                act.wait_ge(used, it * NU + ND)
                act.wait_ge(S["ge_dve"], it)
                act.activation(yhi[:, :], ps[:, 4:6, :].rearrange("p b c -> p (b c)"), ACT.Copy, scale=ge[:, 0:1]).then_inc(S["yhi_done"], 1)

            def expert(it):
                first = isinstance(it, int) and it == 0

                def h_(c):
                    _, g, k0, kt, w = EU[c]
                    act.wait_ge(raw_in[c % NRAW], it * (16 * NU // NRAW) + landed(ND - NRAW + c % NRAW) + 16 * (c // NRAW + 1))
                    act.wait_ge(used, it * NU + ND + c - NHI + 1)
                    act.activation(whi[:, c % NHI, 0:kt * w], raw[:, c % NRAW, 0:kt * w], ACT.Copy).then_inc(hi_done, 1)

                def silu(g, c):
                    act.wait_ge(used, it * NU + ND + c + 1)
                    if not (first and g == 0):
                        act.wait_ge(S["hm_done"], it * 3 + g)
                    act.activation(sgm[:, 0:FGW[g]], bank(2 * (g % 2), FGW[g]), ACT.Silu).then_inc(S["sgm_done"], 1)

                def f_high(g, b):
                    act.wait_ge(S["fT_ps"], it * 3 + g + 1)
                    w = FGW[g]
                    act.activation(fhi[:, g % 2, 0:w // P, :], bank(b, w).rearrange("p (k c) -> p k c", k=w // P), ACT.Copy).then_inc(S["fhi_done"], 1)

                h_(0)
                take_turned(it)
                h_(1)
                if not first:
                    y_high(it)
                h_(2)
                h_(3)
                silu(0, 1)
                for c in range(4, 9):
                    h_(c)
                f_high(0, 6)
                h_(9)
                act.wait_ge(S["mg_used"], it + 1)
                act.activation(selT[:, :], bank(7, T), ACT.Copy).then_inc(S["selT_done"], 1)
                silu(1, 5)
                for c in range(10, 15):
                    h_(c)
                f_high(1, 7)
                silu(2, 11)
                for c in range(15, 18):
                    h_(c)
                f_high(2, 2)
                take_rows(it + 1)

            take_rows(0)
            expert(0)
            with act.Fori(1, NE) as e:
                expert(e)
            act.wait_ge(S["rounds"], 1)
            nr = act.value_load(cnti[0:1, 0:1], min_val=1, max_val=3)
            with act.If(nr > 1):
                with act.Fori(1, nr) as r:
                    with act.Fori(0, NE) as e:
                        expert(r * NE + e)
                y_high(nr * NE)
            with act.Else():
                y_high(NE)
            token_norm(4)
            act.wait_ge(S["col_done"], 4)
            act.wait_ge(S["tT_ps"], 4)
            for half in range(2):
                last = act.activation(yrow[:, 0, half * PB:(half + 1) * PB], token_rows(0, half, P), ACT.Copy, scale=rcol[:, 0:1])
            last.then_inc(S["yr_act"], 1)

        @block.vector
        def _(dve):
            steps = [0]

            def step(ins):
                steps[0] += 1
                ins.then_inc(S["dve_step"], 1)

            def settle(back=0):
                dve.wait_ge(S["dve_step"], steps[0] - back)

            def lo(u):
                _, _, _, w, ks = UNITS[u]
                dve.wait_ge(hi_done, u + 1)
                n = len(ks) * w * (4 - POOL_QUARTERS.get(u, 0)) // 4
                split_low(dve, u, slice(0, n)).then_inc(lo_done, 1)

            def norm_low(n, half):
                dve.wait_ge(S["norm_hi"], 2 * n + half + 1)
                for k in range(4 * half, 4 * half + 4):
                    last = dve.scalar_tensor_tensor(nlo[:, k, :], xT[:, k, :], N_(k, NORM_ROW[n]), nhi[:, k, :].bitcast(F32), ALU.mult, ALU.subtract)
                last.then_inc(S["norm_lo"], 1)

            def norm_rms(n):
                dve.wait_ge(S["norm_rt"], n + 1)
                step(dve.reciprocal(rstd[:, 0, :], rstd[:, 0, :]))

            def token_gain(n, half):
                for k in range(4 * half, 4 * half + 4):
                    last = dve.tensor_scalar(n32[:, k, :], xT[:, k, :], N_(k, NORM_ROW[n]), None, ALU.mult)
                last.then_inc(S["norm_y"], 1)

            def token_rms(n):
                dve.wait_ge(S["norm_rt"], 3 + 2 * (n - 2))
                dve.reciprocal(rcol[:, 0:2], rcol[:, 0:2]).then_inc(S["col_done"], 1)
                dve.reciprocal(rcol[0:NB, 2:3], rcol[0:NB, 2:3]).then_inc(S["col_done"], 1)
                dve.wait_ge(S["col_done"], 2 * (n - 2))

            def scaled(dst, b, planes):
                return dve.tensor_tensor(dst, ps[:, b:b + planes, 0:T], rstd[:, :, :].to_broadcast([P, planes, T]), ALU.mult)

            def taps(src, dst, planes, weight, bias, first, end, onto=False):
                for j in range(first, end):
                    for i in range(planes):
                        if j == first and not onto:
                            step(dve.tensor_scalar(dst[:, i, 0:TP], src[:, i, j:j + TP], weight(j, i), bias(i), ALU.mult, ALU.add))
                        else:
                            settle(planes - 1)
                            step(dve.scalar_tensor_tensor(dst[:, i, 0:TP], src[:, i, j:j + TP], weight(j, i), dst[:, i, 0:TP], ALU.mult, ALU.add))

            def taps_samples(src, dst, planes, width, state, weights, last_weight, bias):
                k = width - 1
                for i in range(planes):
                    o = i * 96 if k < 30 else 0
                    pv = smp[:, o:o + NB * k].rearrange("p (b k) -> p b k", k=k)
                    wv = weights(i).rearrange("p (o k) -> p o k", o=1).to_broadcast([P, NB, k])
                    if k >= 30:
                        settle()
                    step(dve.tensor_tensor(pv, state(i).rearrange("p (b k) -> p b k", k=k), wv, ALU.mult))
                    if k >= 30:
                        settle()
                        step(dve.tensor_reduce(red[:, i, :], pv, AX.X, ALU.add))
                if k < 30:
                    settle()
                    for i in range(planes):
                        pv = smp[:, i * 96:i * 96 + NB * k].rearrange("p (b k) -> p b k", k=k)
                        step(dve.tensor_reduce(red[:, i, :], pv, AX.X, ALU.add))
                for i in range(planes):
                    step(dve.tensor_scalar(dst[:, i, TP:T], src[:, i, k + TP:k + T], last_weight(i), bias(i), ALU.mult, ALU.add))
                settle()
                return dve.tensor_tensor(dst[:, 0:planes, TP:T], dst[:, 0:planes, TP:T], red[:, 0:planes, :], ALU.add)

            dve.wait_ge(S["start_T"], 8)
            dve.tensor_copy(xT[:, 4:8, :], ps[:, 4:8, 0:T]).then_inc(S["start_dve"], 1)

            def parameters_out():
                dve.wait_ge(S["start_T"], 11)
                dve.tensor_copy(prmB[:, :, :], bank(6, 8 * RB).rearrange("p (i r) -> p i r", i=4)).then_inc(S["start_dve"], 1)
                dve.wait_ge(S["start_act"], 4)
                lam = prm[:, PC0:PS0].rearrange("p (i l r) -> p i l r", i=2, l=2)[:, :, :, 7]
                L = [lam_t[:, k, :] for k in range(6)]
                lam4 = lambda t: t.rearrange("p (i l) -> p i l", i=2)
                dve.scalar_tensor_tensor(lam4(L[0]), lam, -1.0, lam, ALU.mult, ALU.max).then_inc(S["lam_abs"], 1)
                step(dve.tensor_scalar(lam4(L[5]), lam, 0.0, None, ALU.min))
                dve.wait_ge(S["lam_exp"], 1)
                step(dve.tensor_scalar(L[2], L[1], 2.0, None, ALU.add))
                settle()
                step(dve.reciprocal(L[2], L[2]))
                settle()
                step(dve.tensor_tensor(L[1], L[1], L[2], ALU.mult))
                settle()
                step(dve.tensor_tensor(L[3], L[1], L[1], ALU.mult))
                settle()
                step(dve.tensor_scalar(L[4], L[3], 1.0 / 17, None, ALU.mult))
                for n in (15, 13, 11, 9, 7, 5, 3):
                    settle()
                    step(dve.scalar_tensor_tensor(L[4], L[4], 1.0 / n, L[3], ALU.add, ALU.mult))
                settle()
                step(dve.scalar_tensor_tensor(L[4], L[4], 1.0, L[1], ALU.add, ALU.mult))
                settle()
                step(dve.scalar_tensor_tensor(L[4], L[4], -2.0, L[5], ALU.mult, ALU.add))
                settle()
                for kind, f in ((0, 8.0), (1, -8.0)):
                    last = dve.tensor_scalar(c8[:, kind, :, :], lam4(L[4]), f, None, ALU.mult)
                last.then_inc(S["lam_done"], 1)
                dve.wait_ge(S["const_done"], 2)

            def layer(l):
                U = FIRST_UNIT[20 * l]
                if l == 0:
                    dve.wait_ge(S["start_act"], 2)
                    norm_low(0, 0)
                    lo(U)
                    dve.wait_ge(S["start_dve"], 1)
                norm_low(2 * l, 1)
                if l == 0:
                    lo(U + 1)
                lo(U + 2)
                norm_rms(2 * l)
                lo(U + 3)
                if l == 0:
                    parameters_out()
                dve.wait_ge(used, U + 2)
                dve.wait_ge(S["pads"], 6 * (l + 1))
                settle()
                scaled(sga[:, :, :], 2, 2).then_inc(S["ga_in"], 1)
                scaled(apad[:, :, 30:30 + T], 0, 2).then_inc(free[0], 1)
                dve.wait_ge(S["sga_done"], l + 1)
                dve.wait_ge(free[0], 1 + 10 * l)
                dve.tensor_tensor(apad[:, :, 30:30 + T], apad[:, :, 30:30 + T], sga[:, :, :], ALU.mult).then_inc(S["apad_done"], 1)
                lo(U + 4)
                lo(U + 5)
                dve.wait_ge(used, U + 4)
                scaled(xbp[:, :, 3:3 + T], 4, 4).then_inc(free[1], 1)
                dve.wait_ge(free[1], 1 + 10 * l)
                taps(xbp, cb, H, lambda j, i: B_(l, j, i), lambda i: B_(l, 4, i), 0, CB)
                taps_samples(xbp, cb, H, CB, lambda i: B_(l, 7, i, 24), lambda i: B_(l, 0, i, 3), lambda i: B_(l, 3, i),
                             lambda i: B_(l, 4, i)).then_inc(S["cb_conv"], 1)
                dve.wait_ge(used, U + 6)
                scaled(gg[:, :, :], 2, 2).then_inc(S["gg_in"], 1)
                scaled(xcp[:, :, 3:3 + T], 0, 2).then_inc(free[0], 1)
                dve.wait_ge(free[0], 2 + 10 * l)
                taps(xcp, xcv, 2, lambda j, i: C_(l, j, i), lambda i: C_(l, 4, i), 0, CC)
                dve.wait_ge(S["cb_conv"], l + 1)
                taps_samples(xcp, xcv, 2, CC, lambda i: C_(l, 16, i, 24), lambda i: C_(l, 0, i, 3), lambda i: C_(l, 3, i),
                             lambda i: C_(l, 4, i)).then_inc(S["xcv_done"], 1)
                lo(U + 6)
                dve.wait_ge(S["xcv_done"], l + 1)
                dve.wait_ge(S["apad_done"], l + 1)
                taps_samples(apad, ac, 2, CA, lambda i: SA[:, i, 240 * l:240 * (l + 1)],
                             lambda i: prm[:, PA0 + i * 2 * RA + l * RA:PA0 + i * 2 * RA + l * RA + 30],
                             lambda i: A_(l, 30, i), lambda i: A_(l, 31, i)).then_inc(S["conv_a_done"], 1)
                tmp, sq = rg_temp(0), rg_temp(1)
                dve.wait_ge(S["ri_done"], 4 * (l + 1))
                step(dve.tensor_tensor(ix[:, :, :], ix[:, :, :], xcv[:, :, :], ALU.mult))

                def conv_a_taps(part):
                    first, end = DVE_TAPS[part:part + 2]
                    if part > 0:
                        settle()
                    taps(apad, ac, 2, lambda j, i: A_(l, j, i), lambda i: A_(l, 31, i), first, end, onto=part > 0)

                conv_a_taps(0)
                r = lambda k, c=slice(0, T): rows[:, k, c]
                pr, sa = slice(0, TP), slice(TP, T)
                dve.wait_ge(S["gate_f"], 2 * (l + 1))
                dve.scalar_tensor_tensor(r(2), r(1), -1.0, r(1), ALU.mult, ALU.max).then_inc(S["gate_abs"], 1)
                step(dve.tensor_scalar(r(6), r(1), 0.0, None, ALU.min))
                conv_a_taps(1)
                dve.wait_ge(S["gate_ln"], l + 1)
                settle()
                step(dve.tensor_tensor(r(6), r(6), r(2), ALU.subtract))
                settle()
                step(dve.memset(r(2, pr), 0.0))
                step(dve.tensor_tensor(r(2, sa), r(6, sa), m0[:, l, :], ALU.add))
                step(dve.tensor_tensor_scan(r(3, pr), r(6, pr), r(0, pr), 0.0, ALU.add, ALU.max))
                settle(1)
                step(dve.tensor_tensor_scan(r(1, pr), r(6, pr), r(2, pr), 0.0, ALU.add, ALU.add))
                step(dve.tensor_tensor(r(3, sa), r(2, sa), r(0, sa), ALU.max))
                settle()
                step(dve.tensor_tensor(r(4, pr), r(1, pr), r(3, pr), ALU.subtract))
                step(dve.tensor_tensor(r(5, pr), r(0, pr), r(1, pr), ALU.subtract))
                step(dve.tensor_tensor(r(4, sa), r(2, sa), r(3, sa), ALU.subtract))
                dve.tensor_tensor(r(5, sa), r(0, sa), r(3, sa), ALU.subtract).then_inc(S["rows_done"], 1)
                lo(U + 7)
                conv_a_taps(2)
                dve.wait_ge(S["R_ps"], l + 1)
                dve.tensor_copy(cols[:, 0:2, 0:2, :], ps[:, 3, COLS0:COLS0 + 4 * H].rearrange("p (j r h) -> p j r h", j=2, r=2)).then_inc(S["ct_dve"], 1)
                dve.tensor_copy(cols[0:NB, 2, 0:2, :], ps[0:NB, 3, COLS0 + 4 * H:COLS0 + 6 * H].rearrange("p (r h) -> p r h", r=2)).then_inc(S["ct_dve"], 1)
                mask = tri[:, :, :].to_broadcast([P, H, P])
                dve.tensor_tensor(E[:, :, 0:P], ps[:, 0:4, 0:P], mask, ALU.add).then_inc(S["R_dve"], 1)
                dve.tensor_copy(E[:, :, P:TP], ps[:, 0:4, P:TP]).then_inc(S["R_dve"], 1)
                dve.tensor_tensor(E[:, :, TP:384], ps[:, 0:4, P:TP], mask, ALU.add).then_inc(S["R_dve"], 1)
                dve.wait_ge(S["rg_act"], 4 * (l + 1))
                step(dve.tensor_tensor(sq, ra[:, :, :], ra[:, :, :], ALU.mult))
                settle()
                dve.scalar_tensor_tensor(tmp, sq, 1.0, tmp, ALU.add, ALU.mult).then_inc(S["rg_dve"], 1)
                conv_a_taps(3)
                dve.wait_ge(used, U + 8)
                scaled(vT[:, :, :], 4, 4).then_inc(free[1], 1)
                settle()
                dve.wait_ge(S["conv_a_taps"], 2 * (l + 1))
                dve.tensor_tensor(ac[:, :, 0:TP], ac[:, :, 0:TP], pool_taps(vg), ALU.add).then_inc(S["conv_a_done"], 1)
                dve.wait_ge(S["E_done"], l + 1)
                step(dve.tensor_copy(gcol[:, :, :], E[:, :, :].rearrange("p h (c k) -> p h c k", k=P)[:, :, 1:3, P - 1]))
                settle()
                for h in range(H):
                    if h == 2:
                        dve.wait_ge(S["lna_ps"], 2 * l + 1)
                        dve.tensor_tensor(ac[:, :, :], ac[:, :, :], ps[:, 5:7, 0:T], ALU.subtract).then_inc(S["lna_xm"], 1)
                    dve.wait_ge(S["s_ps"], 4 * l + h + 1)
                    last = dve.tensor_tensor(E[:, h, :], E[:, h, :], ps[:, h, 0:384], ALU.mult)
                last.then_inc(S["P_done"], 1)
                for h in range(H):
                    if h == 2:
                        dve.wait_ge(S["lna_rt"], l + 1)
                        dve.reciprocal(sga[:, :, :], sga[:, :, :]).then_inc(S["lna_inv"], 1)
                    if h >= 2:
                        dve.wait_ge(S["cp_ps"], 4 * l + h - 1)
                    dve.tensor_scalar(vg[:, h % 2, 0, :], v1[:, 0, h, :], gcol[:, h, 0:1], None, ALU.mult)
                    dve.tensor_scalar(vg[:, h % 2, 1, :], v1[:, 1, h, :], gcol[:, h, 1:2], None, ALU.mult).then_inc(S["vg_done"], 1)

                ht = E[:, :, :].rearrange("p h c -> p (h c)").rearrange("p (t c) -> p t c", t=3)

                def heads(tiles, n, banks):
                    for j in tiles:
                        b = banks + 2 * j if len(tiles) > 1 else banks
                        den = ps[0:n, b:b + 2, 0:2 * (P + 1)].rearrange("p b (h c) -> p b h c", h=2)[:, :, :, P]
                        low = cols[0:n, j, 2, :].rearrange("p (b h) -> p b h", b=2)
                        hj = hr[0:n, j, :].rearrange("p (b h) -> p b h", b=2)
                        step(dve.scalar_tensor_tensor(hj, den, -1.0, low, ALU.mult, ALU.max))
                        settle()
                        step(dve.tensor_tensor(hj, hj, den, ALU.max))
                    settle()
                    t = slice(tiles[0], tiles[-1] + 1)
                    step(dve.reciprocal(hr[0:n, t, :], hr[0:n, t, :]))
                    settle()
                    for j in tiles:
                        b = banks + 2 * j if len(tiles) > 1 else banks
                        for h in range(H):
                            o = (h % 2) * (P + 1)
                            last = dve.tensor_scalar(ht[0:n, j, h * P:(h + 1) * P], ps[0:n, b + h // 2, o:o + P], hr[0:n, j, h:h + 1], None, ALU.mult)
                    last.then_inc(S["num_read"], 1)

                def heads_statistics(tiles, n, note):
                    dve.wait_ge(S["num_read"], note)
                    for j in tiles:
                        for h in range(H):
                            step(dve.bn_stats(st6[0:n, j, h, :], ht[0:n, j, h * P:(h + 1) * P]))
                    settle()
                    for j in tiles:
                        for h in range(H):
                            last = dve.bn_aggr(mv[0:n, j, h, :], st6[0:n, j, h, :])
                    last.then_inc(S["var_done"], 1)

                def heads_norm(tiles, n, note):
                    dve.wait_ge(S["var_done"], note)
                    dve.wait_ge(S["sd_done"], note)
                    t = slice(tiles[0], tiles[-1] + 1)
                    step(dve.reciprocal(hr[0:n, t, :], hr[0:n, t, :]))
                    settle()
                    for j in tiles:
                        for h in range(H):
                            c = ht[0:n, j, h * P:(h + 1) * P]
                            last = dve.tensor_scalar(c, c, mv[0:n, j, h, 0:1], hr[0:n, j, h:h + 1], ALU.subtract, ALU.mult)
                    return last

                def sample_head(h):
                    n = 4 * l + h
                    dve.wait_ge(S["outer_ps"], n + 1)
                    for b in range(NB):
                        o = (b % 3) * (P + 1)
                        last = dve.scalar_tensor_tensor(Cs[:, h, b, :], Cs[:, h, b, :], dec[:, h, 0, b:b + 1],
                                                        ps[:, outer_bank(h, b // 3), o:o + P + 1], ALU.mult, ALU.add)
                    last.then_inc(S["cs_new"], 1)

                dve.wait_ge(S["num_ps"], l + 1)
                heads((0, 1), P, 4)
                dve.wait_ge(S["cs_in"], 64 * (l + 1))
                dve.wait_ge(S["cs_n"], l + 1)
                sample_head(0)
                heads_statistics((0, 1), P, 2 * l + 1)
                sample_head(1)
                dve.wait_ge(S["rg_sqrt"], l + 1)
                step(dve.tensor_tensor(ix[:, :, :], ix[:, :, :], tmp, ALU.mult))
                settle()
                h0 = prm[:, PC0:PS0].rearrange("p (i l r) -> p i l r", i=2, l=2)[:, :, l, 8:16]
                step(dve.tensor_tensor(xcv[:, :, TP:T], ra[:, :, TP:T], h0, ALU.mult))
                for i in range(2):
                    step(dve.tensor_tensor_scan(xcv[:, i, 0:TP], ra[:, i, 0:TP], ix[:, i, 0:TP], 0.0, ALU.mult, ALU.add))
                settle(2)
                step(dve.tensor_tensor(xcv[:, :, TP:T], xcv[:, :, TP:T], ix[:, :, TP:T], ALU.add))
                settle()
                dve.wait_ge(S["gg_done"], l + 1)
                dve.tensor_tensor(gg[:, :, :], gg[:, :, :], xcv[:, :, :], ALU.mult).then_inc(S["rg_done"], 1)
                sample_head(2)
                step(heads_norm((0, 1), P, 2 * l + 1))
                lo(U + 8)
                dve.wait_ge(S["y_hi"], 3 * l + 1)
                dve.tensor_tensor(nlo[:, 0:2, :], ac[:, :, :], nhi[:, 0:2, :].bitcast(F32), ALU.subtract).then_inc(S["y_lo"], 1)
                dve.wait_ge(S["y_hi"], 3 * l + 2)
                dve.tensor_tensor(nlo[:, 6:8, :], gg[:, :, :], nhi[:, 6:8, :].bitcast(F32), ALU.subtract).then_inc(S["y_lo"], 1)
                sample_head(3)
                dve.wait_ge(S["cs_used"], 4 * (l + 1))
                heads((2,), NB, 4)
                heads_statistics((2,), NB, 2 * l + 2)
                heads_norm((2,), NB, 2 * l + 2).then_inc(S["h_norm"], 1)
                lo(U + 9)
                dve.wait_ge(S["hT_ps"], l + 1)
                dve.wait_ge(S["sk_done"], l + 1)
                for h in range(H):
                    step(dve.scalar_tensor_tensor(cb[:, h, :], bank(4 + h, T), B_(l, 5, h), cb[:, h, :], ALU.mult, ALU.add))
                settle()
                dve.wait_ge(S["sz_done"], l + 1)
                dve.tensor_tensor(cb[:, :, :], cb[:, :, :], vT[:, :, :], ALU.mult).then_inc(S["yb_done"], 1)
                dve.wait_ge(S["y_hi"], 3 * l + 3)
                dve.tensor_tensor(nlo[:, 2:6, :], cb[:, :, :], nhi[:, 2:6, :].bitcast(F32), ALU.subtract).then_inc(S["y_lo"], 1)
                lo(U + 10)
                lo(U + 11)
                dve.wait_ge(used, U + 10)
                dve.tensor_tensor(xT[:, 0:4, :], xT[:, 0:4, :], ps[:, 0:4, 0:T], ALU.add).then_inc(free[0], 1)
                if l == 0:
                    lo(12)
                    lo(13)
                else:
                    dve.wait_ge(S["stored"], 16 * STORES * DEPTH)
                    dve.wait_ge(free[0], TAKEN[3])
                    token_gain(3, 0)
                dve.wait_ge(used, U + 12)
                dve.tensor_tensor(xT[:, 4:8, :], xT[:, 4:8, :], ps[:, 4:8, 0:T], ALU.add).then_inc(free[1], 1)

            layer(0)
            norm_low(1, 0)
            norm_low(1, 1)
            norm_rms(1)
            for g in range(6):
                u, n = 12 + 4 * g, GROUPS[6 + 2 * g][3] // P
                lo(u + 2)
                dve.wait_ge(used, u + 2)
                if g == 0:
                    settle()
                else:
                    dve.wait_ge(S["hlo_done"], g)
                scaled(sg[:, 0:n, :], 0, n).then_inc(free[0], 1)
                lo(u + 3)
                dve.wait_ge(S["silu_done"], g + 1)
                step(dve.tensor_tensor(sg[:, 0:n, :], sg[:, 0:n, :], rstd[:, :, :].to_broadcast([P, n, T]), ALU.mult))
                lo(u + 4)
                lo(u + 5)
                settle()
                dve.wait_ge(used, u + 4)
                dve.tensor_tensor(sg[:, 0:n, :], sg[:, 0:n, :], ps[:, 4:4 + n, 0:T], ALU.mult).then_inc(free[1], 1)
                dve.wait_ge(S["hhi_done"], g + 1)
                dve.tensor_tensor(hlo[:, 4 * g:4 * g + n, :], sg[:, 0:n, :], hhi[:, 4 * g:4 * g + n, :].bitcast(F32), ALU.subtract).then_inc(S["hlo_done"], 1)
            for g in range(2):
                for u in (range(38, 44), range(44, 48))[g]:
                    lo(u)
                if g == 1:
                    norm_low(2, 0)
                    lo(48)
                dve.wait_ge(used, 42 + 6 * g)
                dve.tensor_tensor(xT[:, 4 * g:4 * g + 4, :], xT[:, 4 * g:4 * g + 4, :], ps[:, 4 * g:4 * g + 4, 0:T], ALU.add).then_inc(free[g], 1)
            lo(49)
            layer(1)
            dve.wait_ge(free[1], TAKEN[3])
            token_gain(3, 1)
            token_rms(3)
            step(dve.tensor_copy(biases[:, :], ps[:, 0, BI0:BI0 + NE]))
            settle()

            dve.wait_ge(S["moe_const"], 3)
            dve.wait_ge(S["cs_out"], 64 * DEPTH)
            for j, (_, n) in enumerate(TILES):
                step(dve.scalar_tensor_tensor(lg[0:n, j, :], ps[0:n, 0, LG0 + j * (NE + 1):LG0 + j * (NE + 1) + NE], rcol[0:n, j:j + 1],
                                              biases[0:n, :], ALU.mult, ALU.add))
            settle()
            for j, (_, n) in enumerate(TILES):
                step(dve.max(top[0:n, j, :], lg[0:n, j, :]))
            settle()
            for j, (_, n) in enumerate(TILES):
                step(dve.max_index(topi[0:n, j, :], top[0:n, j, :], lg[0:n, j, :]))
                dve.tensor_tensor(gt[0:n, j, 0:1], top[0:n, j, 1:2], top[0:n, j, 0:1], ALU.subtract).then_inc(S["top_done"], 1)
            settle()
            for j, (_, n) in enumerate(TILES):
                step(dve.tensor_copy(topf[0:n, j, :], topi[0:n, j, 0:2]))
            settle()
            for j, (_, n) in enumerate(TILES):
                for i in range(2):
                    step(dve.tensor_scalar(oh[0:n, j, i, :], iota[0:n, 0:NE], topf[0:n, j, i:i + 1], None, ALU.is_equal))
            dve.wait_ge(S["gate_exp"], 3)
            for j, (_, n) in enumerate(TILES):
                step(dve.tensor_scalar(gt[0:n, j, 2:3], gt[0:n, j, 1:2], 1.0, None, ALU.add))
            settle()
            for j, (_, n) in enumerate(TILES):
                step(dve.reciprocal(gt[0:n, j, 2:3], gt[0:n, j, 2:3]))
            settle()
            for j, (_, n) in enumerate(TILES):
                step(dve.tensor_tensor(gt[0:n, j, 3:4], gt[0:n, j, 1:2], gt[0:n, j, 2:3], ALU.mult))
                step(dve.tensor_scalar(comb[0:n, j, :], oh[0:n, j, 0, :], gt[0:n, j, 2:3], None, ALU.mult))
                step(dve.tensor_tensor(chosen[0:n, j, 0:NE], oh[0:n, j, 0, :], oh[0:n, j, 1, :], ALU.add))
            settle()
            for j, (_, n) in enumerate(TILES):
                step(dve.tensor_copy(chosen[0:n, j, NE:NE + 1], chosen[0:n, j, 0:1]))
                last = dve.scalar_tensor_tensor(comb[0:n, j, :], oh[0:n, j, 1, :], gt[0:n, j, 3:4], comb[0:n, j, :], ALU.mult, ALU.add)
            last.then_inc(S["route_done"], 1)
            for j, (_, n) in enumerate(TILES):
                for half in range(2):
                    c = slice(half * PB, (half + 1) * PB)
                    dve.wait_ge(S["tT_hi"], 2 * j + half + 1)
                    dve.scalar_tensor_tensor(tlo[0:n, j, c], token_rows(j, half, n), rcol[0:n, j:j + 1], thi[0:n, j, c].bitcast(F32),
                                             ALU.mult, ALU.subtract).then_inc(S["tT_lo"], 1)
            dve.wait_ge(S["tT_hi"], 7)
            for j, (_, n) in enumerate(TILES):
                step(dve.tensor_tensor(thi[0:n, j, D + NE:D + 2 * NE], comb[0:n, j, :], thi[0:n, j, D:D + NE].bitcast(F32), ALU.subtract))
            dve.wait_ge(S["rk_ps"], 1)
            for j, (_, n) in enumerate(TILES):
                step(dve.tensor_copy(rank[0:n, j, 0:NE], ps[0:n, 0, j * NE:(j + 1) * NE]))
                step(dve.tensor_scalar(rank[0:n, j, NE:NE + 1], ps[0:n, 0, j * NE:j * NE + 1], float(P), None, ALU.subtract))
            step(dve.tensor_reduce(cnt[:, 0:1], ps[:, 0, 3 * NE:4 * NE], AX.X, ALU.max))
            settle()
            step(dve.tensor_scalar(cnt[:, 1:2], cnt[:, 0:1], float(P), 1.0, ALU.is_gt, ALU.add))
            settle()
            step(dve.scalar_tensor_tensor(cnt[:, 2:3], cnt[:, 0:1], float(2 * P), cnt[:, 1:2], ALU.is_gt, ALU.add))
            settle()
            dve.wait_ge(S["moe_const"], 4)
            dve.tensor_copy(cnti[:, :], cnt[:, 2:3]).then_inc(S["rounds"], 1)

            def choose(it, e):
                for j, (_, n) in enumerate(TILES):
                    dve.tensor_scalar(sel[0:n, j, :], iota[0:n, :], rank[0:n, j, bass.ds(e, 1)], chosen[0:n, j, bass.ds(e, 1)],
                                      ALU.is_equal, ALU.mult).then_inc(S["sel_done"], 1)

            def turned_low(it):
                dve.wait_ge(S["ehi_done"], it + 1)
                dve.tensor_tensor(elo[:, :, :], ps[:, 6:8, :].rearrange("p b (k c) -> p (b k) c", k=4), ehi[:, :, :].bitcast(F32),
                                  ALU.subtract).then_inc(S["elo_done"], 1)

            def y_low(it):
                dve.wait_ge(S["yhi_done"], it + 1)
                dve.scalar_tensor_tensor(ylo[:, :], ps[:, 4:6, :].rearrange("p b c -> p (b c)"), ge[:, 0:1], yhi[:, :].bitcast(F32),
                                         ALU.mult, ALU.subtract).then_inc(S["ylo_done"], 1)

            def add_rows(it, pair, done=None):
                dve.wait_ge(S["sc_ps"], it * 4 + pair + 1)
                c = slice(2 * pair, 2 * pair + 2)
                if pair == 0 and not (isinstance(it, int) and it == 0):
                    dve.wait_ge(S["x_add"], it * 4)
                dve.tensor_tensor(xT[:, c, :], xT[:, c, :], ps[:, 6:8, 0:T], ALU.add).then_inc(S["x_add"] if done is None else done, 1)

            def expert(it, e, moved=None):
                first = isinstance(it, int) and it == 0

                def l_(c):
                    _, g, k0, kt, w = EU[c]
                    dve.wait_ge(hi_done, it * NU + ND + c + 1)
                    split_low(dve, c, slice(0, kt * w * 3 // 4)).then_inc(lo_done, 1)

                def product(g, c):
                    dve.wait_ge(S["sgm_done"], it * 3 + g + 1)
                    dve.wait_ge(used, it * NU + ND + c + 1)
                    if not (first and g < 2):
                        dve.wait_ge(S["fT_ps"], it * 3 + g - 1 if g < 2 else it * 3 + 1)
                    dve.tensor_tensor(hm[:, g % 2, 0:FGW[g]], sgm[:, 0:FGW[g]], bank(2 * (g % 2) + 1, FGW[g]), ALU.mult).then_inc(S["hm_done"], 1)

                def f_low(g, b):
                    w = FGW[g]
                    dve.wait_ge(S["fhi_done"], it * 3 + g + 1)
                    dve.tensor_tensor(flo[:, g % 2, 0:w // P, :], bank(b, w).rearrange("p (k c) -> p k c", k=w // P),
                                      fhi[:, g % 2, 0:w // P, :].bitcast(F32), ALU.subtract).then_inc(S["flo_done"], 1)

                l_(0)
                turned_low(it)
                l_(1)
                if not first:
                    y_low(it)
                l_(2)
                l_(3)
                add_rows(it, 0)
                l_(4)
                add_rows(it, 1)
                l_(5)
                product(0, 3)
                add_rows(it, 2)
                l_(6)
                add_rows(it, 3)
                l_(7)
                l_(8)
                f_low(0, 6)
                l_(9)
                dve.wait_ge(S["mg_used"], it + 1)
                dve.wait_ge(S["selT_done"], it + 2)
                dve.tensor_copy(ge[:, 0:1], ps[:, 7, bass.ds(e + 272, 1)]).then_inc(S["ge_dve"], 1)
                if moved is not None:
                    dve.wait_ge(S["ranks_moved"], moved)
                choose(it + 1, e + 1)
                l_(10)
                product(1, 7)
                for c in range(11, 15):
                    l_(c)
                f_low(1, 7)
                l_(15)
                product(2, 13)
                l_(16)
                l_(17)
                f_low(2, 2)

            settle()
            choose(0, 0)
            expert(0, 0)
            with dve.Fori(1, NE) as e:
                expert(e, e)
            nr = dve.value_load(cnti[0:1, 0:1], min_val=1, max_val=3)
            with dve.If(nr > 1):
                with dve.Fori(1, nr) as r:
                    for j, (_, n) in enumerate(TILES):
                        last = dve.tensor_scalar(rank[0:n, j, :], rank[0:n, j, :], float(P), None, ALU.subtract)
                    last.then_inc(S["ranks_moved"], 1)
                    with dve.Fori(0, NE) as e:
                        expert(r * NE + e, e, r)
                y_low(nr * NE)
                for pair in range(4):
                    add_rows(nr * NE, pair, S["x_new"] if pair == 3 else None)
            with dve.Else():
                y_low(NE)
                for pair in range(4):
                    add_rows(NE, pair, S["x_new"] if pair == 3 else None)
            dve.wait_ge(S["x_new"], 1)
            token_gain(4, 0)
            token_gain(4, 1)
            token_rms(4)
            dve.wait_ge(S["tT_ps"], 4)
            for j in (1, 2):
                n = TILES[j][1]
                for half in range(2):
                    last = dve.tensor_scalar(yrow[0:n, j, half * PB:(half + 1) * PB], token_rows(j, half, n), rcol[0:n, j:j + 1], None, ALU.mult)
                last.then_inc(S["yr_dve"], 1)

        @block.gpsimd
        def _(pool):
            steps = [0]

            def step(ins):
                steps[0] += 1
                ins.then_inc(S["pool_step"], 1)

            def settle(back=0):
                pool.wait_ge(S["pool_step"], steps[0] - back)

            step(pool.memset(ident[:, :], 0.0))
            settle()
            pool.affine_select(out=ident[:, :], in_=ident[:, :], compare_op=ALU.not_equal, fill=1.0, base=0,
                               pattern=[[-1, P]], channel_multiplier=1).then_inc(S["const_done"], 1)
            step(pool.memset(ones[:, :], 1.0))
            step(pool.memset(gmean[:, :], 0.0))
            step(pool.memset(tri[:, :, :], 0.0))
            step(pool.memset(eye8[:, :, :], 0.0))
            settle()
            step(pool.memset(gmean[0:64, 0:64], 1.0 / 64))
            settle()
            step(pool.memset(gmean[64:128, 64:128], 1.0 / 64))
            settle()
            step(pool.affine_select(out=tri[:, 0, :], in_=tri[:, 0, :], compare_op=ALU.is_ge, fill=NEG, base=0,
                                    pattern=[[1, P]], channel_multiplier=-1))
            step(pool.affine_select(out=eye8[:, :, :], in_=eye8[:, :, :], compare_op=ALU.not_equal, fill=1.0, base=0,
                                    pattern=[[1, NB], [-1, NB]], channel_multiplier=0))
            settle()
            pool.memset(rstd[:, 0, 0:1], 0.0).then_inc(S["const_done"], 1)
            step(pool.memset(unit9[:, :], 0.0))
            step(pool.memset(wrt[:, :, :], 0.0))
            settle()
            pool.memset(unit9[:, NE:NE + 1], 1.0).then_inc(S["moe_const"], 1)
            pool.dma_start(wrt[:, :, 0:NE], a["w_router"][0].rearrange("(k p) e -> p k e", p=P)).then_inc(S["router_in"], 16)
            pool.dma_start(brt[:, :], a["b_router"]).then_inc(S["router_in"], 16)
            pool.iota(iota[:, :], pattern=[[1, P]], base=0, channel_multiplier=0, allow_small_or_imprecise_dtypes=True).then_inc(S["moe_const"], 1)
            step(pool.memset(before[:, :], 1.0))
            settle()
            pool.affine_select(out=before[:, :], in_=before[:, :], compare_op=ALU.is_ge, fill=0.0, base=-1,
                               pattern=[[1, P]], channel_multiplier=-1).then_inc(S["moe_const"], 1)

            def lo(u):
                n = UNITS[u][3] * len(UNITS[u][4])
                pool.wait_ge(hi_done, u + 1)
                split_low(pool, u, slice(n * (4 - POOL_QUARTERS[u]) // 4, n)).then_inc(lo_pool, 1)

            def layer(l):
                if l == 0:
                    pool.wait_ge(S["start_T"], 12)
                    pool.wait_ge(S["lam_done"], 1)
                else:
                    pool.wait_ge(free[0], 10)
                    pool.wait_ge(free[1], 10)
                pool.memset(apad[:, :, 0:30], 0.0).then_inc(S["pads"], 1)
                pool.memset(xbp[:, :, 0:3], 0.0).then_inc(S["pads"], 1)
                pool.memset(xcp[:, :, 0:3], 0.0).then_inc(S["pads"], 1)
                pool.memset(v1[:, :, :, P:P + 1], 1.0).then_inc(S["pads"], 1)
                pool.memset(wg[:, :, :], 0.0).then_inc(S["pads"], 1)
                pool.memset(wr[:, :, :, :], 0.0).then_inc(S["pads"], 1)
                for h in range(H):
                    pool.dma_start(Cs[:, h, :, 0:P], a["state_mlstm_C"][l, :, h].rearrange("b k v -> k b v")).then_inc(S["cs_in"], 16)
                n_old = prm[:, PS0 + l * NB * H:PS0 + (l + 1) * NB * H].rearrange("p (b h o) -> p h b o", h=H, o=1)
                pool.tensor_copy(Cs[:, :, :, P:P + 1], n_old).then_inc(S["cs_n"], 1)
                pool.wait_ge(S["apad_done"], l + 1)
                total, product = pool_taps(vg), pool_taps(Cp)
                for i in range(2):
                    step(pool.tensor_scalar(total[:, i, :], apad[:, i, 0:TP], A_(l, 0, i), None, ALU.mult))
                for j in range(1, POOL_TAPS):
                    for i in range(2):
                        settle(1)
                        step(pool.tensor_scalar(product[:, i, :], apad[:, i, j:j + TP], A_(l, j, i), None, ALU.mult))
                    for i in range(2):
                        settle(1 if j < POOL_TAPS - 1 else 1 - i)
                        ins = pool.tensor_tensor(total[:, i, :], total[:, i, :], product[:, i, :], ALU.add)
                        if j < POOL_TAPS - 1:
                            step(ins)
                        else:
                            ins.then_inc(S["conv_a_taps"], 1)
                pool.wait_ge(S["q_out"], l + 1)
                for h in range(H):
                    qs = qT[:, h, TP:T].rearrange("p (o b) -> p o b", o=1).to_broadcast([P, NB, NB])
                    pool.tensor_tensor(Qm[:, h, :, :], qs, eye8[:, :, :], ALU.mult).then_inc(S["Qm_done"], 1)
                pool.wait_ge(S["em_done"], 3 * (l + 1))
                pool.tensor_tensor(gsm[:, :, :], ident[0:NB, 0:NB].rearrange("p (o b) -> p o b", o=1).to_broadcast([NB, H, NB]),
                                   gs[:, :].rearrange("p (h o) -> p h o", o=1).to_broadcast([NB, H, NB]), ALU.mult).then_inc(S["gsm_done"], 1)
                pool.wait_ge(S["gsm_done"], l + 1)
                pool.wait_ge(S["v1_done"], 3 * (l + 1))
                pool.wait_ge(S["P_done"], l + 1)
                pool.wait_ge(S["Qm_done"], 4 * (l + 1))
                pool.wait_ge(S["ktok_done"], 3 * (l + 1))
                for h in range(H):
                    if h == 2:
                        pool.wait_ge(S["lna_inv"], l + 1)
                        pool.tensor_tensor(ac[:, :, :], ac[:, :, :], sga[:, :, :], ALU.mult).then_inc(S["lna_done"], 1)
                    if h >= 2:
                        pool.wait_ge(S["outer_ps"], 4 * l + h - 1)
                    pool.tensor_tensor(value_rows(h).rearrange("p (b c) -> p b c", b=NB),
                                       v1[0:NB, 2, h, :].rearrange("p (o c) -> p o c", o=1).to_broadcast([NB, NB, P + 1]),
                                       gsm[:, h, :].rearrange("p (b o) -> p b o", o=1).to_broadcast([NB, NB, P + 1]),
                                       ALU.mult).then_inc(S["Vm_done"], 1)
                pool.wait_ge(S["cp_out"], l + 1)
                pool.dma_start(out["C_p"][l, 0].rearrange("h k v -> k h v"), Cp[:, :, 0:P]).then_inc(S["stored"], 16)
                pool.dma_start(out["m_p"][l], cols[P - 1:P, 1, 1, :]).then_inc(S["stored"], 16)
                pool.dma_start(out["m_s"][l], cols[0:NB, 2, 1, :]).then_inc(S["stored"], 16)
                for u in range(FIRST_UNIT[20 * l + 4], FIRST_UNIT[20 * l + 4] + 3):
                    lo(u)
                pool.wait_ge(S["cs_new"], 4 * (l + 1))
                pool.tensor_copy(smp[:, 400:432].rearrange("p (b h o) -> p h b o", h=H, o=1), Cs[:, :, :, P:P + 1]).then_inc(S["ns_done"], 1)
                for h in range(H):
                    pool.dma_start(out["C_s"][l, :, h].rearrange("b k v -> k b v"), Cs[:, h, :, 0:P]).then_inc(S["cs_out"], 16)
                dests = [[(0, 30, out["conv_a_p"][l, 0]), (30, 38, out["conv_a_s"][l, :, 29, :])],
                         [(0, 3, out["conv_b_p"][l, 0]), (3, 11, out["conv_b_s"][l, :, 2, :])],
                         [(0, 3, out["conv_c_p"][l, 0]), (3, 11, out["conv_c_s"][l, :, 2, :])],
                         [(0, 1, out["h_p"][l]), (1, 9, out["h_s"][l])],
                         [(0, 32, out["n_s"][l].rearrange("b h k -> (b h) k")), (32, 36, out["n_p"][l, 0])]]
                for k, ds_ in enumerate(dests):
                    pool.wait_ge(S["so_out"], 5 * l + k + 1)
                    for r0, r1, dst in ds_:
                        pool.dma_start(dst, so_tile(k)[r0:r1]).then_inc(S["stored"], 16)
                pool.wait_ge(S["stored"], 16 * STORES * (l + 1))
                pool.wait_ge(S["cs_out"], 64 * (l + 1))

            layer(0)
            with nc.allow_non_contiguous_dma(reason="rows of the states"):
                for l in range(DEPTH):
                    for n, w in (("a", CA), ("b", CB), ("c", CC)):
                        pool.dma_start(out[f"conv_{n}_s"][l, :, 0:w - 2, :], a[f"state_conv_{n}"][l, :, 1:w - 1, :]).then_inc(S["copied"], 16)
            for u in POOL_UNITS:
                if FIRST_UNIT[6] <= u < FIRST_UNIT[20]:
                    lo(u)
            layer(1)
            pool.wait_ge(S["copied"], 96)

            pool.wait_ge(free[0], 13)
            pool.wait_ge(free[1], 13)
            pool.memset(yhi[:, :].bitcast(F32), 0.0).then_inc(S["yhi_done"], 1)
            pool.memset(ylo[:, :].bitcast(F32), 0.0).then_inc(S["ylo_done"], 1)
            pool.memset(selT[:, :].bitcast(F32), 0.0).then_inc(S["selT_done"], 1)
            pool.memset(cnti[:, :], 0).then_inc(S["moe_const"], 1)

            def expert(it):
                for c, (_, g, k0, kt, w) in enumerate(EU):
                    pool.wait_ge(hi_done, it * NU + ND + c + 1)
                    split_low(pool, c, slice(kt * w * 3 // 4, kt * w)).then_inc(lo_pool, 1)

            expert(0)
            with pool.Fori(1, NE) as e:
                expert(e)
            pool.wait_ge(S["rounds"], 1)
            nr = pool.value_load(cnti[0:1, 0:1], min_val=1, max_val=3)
            with pool.If(nr > 1):
                with pool.Fori(1, nr) as r:
                    with pool.Fori(0, NE) as e:
                        expert(r * NE + e)


INS = ["x_prompt", "x_sample", "state_conv_a", "state_conv_b", "state_mlstm_C", "state_mlstm_n", "state_mlstm_m", "state_conv_c",
       "state_rglru_h", "norm_mix_g", "w_in", "conv_a_w", "conv_a_b", "ln_a_g", "ln_a_b", "conv_b_w", "conv_b_b", "w_q", "w_k", "w_v",
       "w_ig", "b_ig", "w_fg", "b_fg", "gn_b_g", "skip_b", "conv_c_w", "conv_c_b", "w_ra", "b_ra", "w_ix", "b_ix", "lam", "w_out",
       "norm_ffn_g", "w_gate", "w_up", "w_down", "w_router", "b_router", "we_gate", "we_up", "we_down", "norm_final_g"]
OUTS = [("y_p", (1, TP, D)), ("y_s", (NB, 1, D)),
        ("conv_a_p", (DEPTH, 1, CA - 1, 256)), ("conv_b_p", (DEPTH, 1, CB - 1, 512)), ("C_p", (DEPTH, 1, H, P, P)), ("n_p", (DEPTH, 1, H, P)),
        ("m_p", (DEPTH, 1, H)), ("conv_c_p", (DEPTH, 1, CC - 1, 256)), ("h_p", (DEPTH, 1, 256)),
        ("conv_a_s", (DEPTH, NB, CA - 1, 256)), ("conv_b_s", (DEPTH, NB, CB - 1, 512)), ("C_s", (DEPTH, NB, H, P, P)), ("n_s", (DEPTH, NB, H, P)),
        ("m_s", (DEPTH, NB, H)), ("conv_c_s", (DEPTH, NB, CC - 1, 256)), ("h_s", (DEPTH, NB, 256))]


def kernel(**inputs):
    import concourse.bacc as bacc
    from concourse.bass_utils import run_bass_kernel_spmd

    nc = bacc.Bacc("TRN2", target_bir_lowering=False, num_devices=1)
    arrays = {"in_" + n: np.ascontiguousarray(inputs[n]) for n in INS}
    ins = {n: nc.dram_tensor("in_" + n, arrays["in_" + n].shape, F32, kind="ExternalInput").ap() for n in INS}
    outs = {n: nc.dram_tensor("out_" + n, shape, F32, kind="ExternalOutput").ap() for n, shape in OUTS}
    build(nc, ins, outs)
    r = run_bass_kernel_spmd(nc, [arrays], core_ids=[0])
    return tuple(r.results[0]["out_" + n] for n, _ in OUTS)
```
